# Optimizing a Trainium2 kernel written in Bass

```python
import math
import jax, jax.numpy as jnp
from jax import lax
import numpy as np

D_MODEL = 1024
BATCH = 1
SEQ = 512
DEPTH = 1
DEC_BATCH = 8
DEC_SEQ = 4
PAST_LEN = 2048
PAGE_SIZE = 128

N_META = 16
MLA_HEADS = 8
QK_NOPE = 64
QK_ROPE = 32
V_DIM = 64
Q_RANK = 256
KV_RANK = 128
ROPE_THETA = 10000.0
Q_BLOCK = 128
SM_SCALE = (QK_NOPE + QK_ROPE) ** -0.5
ML_HEADS = 4
ML_DH = 128
ML_W = ML_HEADS * ML_DH
CHUNK = 64
MLA_W = MLA_HEADS * V_DIM
MIX_W = MLA_W + ML_W
O_CQ = 0
O_CKV = O_CQ + Q_RANK
O_KR = O_CKV + KV_RANK
O_MQ = O_KR + QK_ROPE
O_MK = O_MQ + ML_W
O_MV = O_MK + ML_W
O_MO = O_MV + ML_W
O_G = O_MO + ML_W
IN_W = O_G + 2 * ML_HEADS
PEER_HEADS = 8
N_KEYS = 128
N_EXPERTS = N_KEYS * N_KEYS
PEER_DQ = 256
PEER_TOPK = 16
PEER_BLOCK = 256
DN_ALPHA = (2.0 * DEPTH) ** 0.25
DN_BETA = (8.0 * DEPTH) ** -0.25
EPS = 1e-5

kernel_name = "hymba_mla_mlstm_peer_step"

def layer_norm(x, g, b):
    xf = x.astype(jnp.float32)
    mu = xf.mean(-1, keepdims=True)
    var = jnp.square(xf - mu).mean(-1, keepdims=True)
    return ((xf - mu) * lax.rsqrt(var + EPS) * g + b).astype(x.dtype)

def rms_norm(x, g):
    xf = x.astype(jnp.float32)
    return (xf * lax.rsqrt(jnp.square(xf).mean(-1, keepdims=True) + 1e-6) * g).astype(x.dtype)

def rope(x, pos):
    half = QK_ROPE // 2
    inv = ROPE_THETA ** (-jnp.arange(half, dtype=jnp.float32) / half)
    ang = pos.astype(jnp.float32)[:, None] * inv
    ang = ang.reshape((ang.shape[0],) + (1,) * (x.ndim - 3) + (half,))
    cos, sin = jnp.cos(ang), jnp.sin(ang)
    xf = x.astype(jnp.float32)
    x1, x2 = xf[..., :half], xf[..., half:]
    return jnp.concatenate([x1 * cos - x2 * sin, x1 * sin + x2 * cos], axis=-1).astype(x.dtype)

def mixer_project(h, pos, w_in, b_gates, q_norm_g, w_qb, kv_norm_g, w_kvb):
    B, T, _ = h.shape
    z = jnp.einsum('btd,de->bte', h, w_in)
    c_q = z[..., O_CQ:O_CKV]
    c_kv = z[..., O_CKV:O_KR]
    k_r = z[..., O_KR:O_MQ]
    q = jnp.einsum('btr,re->bte', rms_norm(c_q, q_norm_g), w_qb).reshape(B, T, MLA_HEADS, QK_NOPE + QK_ROPE)
    q_nope, q_rope = q[..., :QK_NOPE], rope(q[..., QK_NOPE:], pos)
    w_uk = w_kvb.reshape(KV_RANK, MLA_HEADS, QK_NOPE + V_DIM)[..., :QK_NOPE]
    q_lat = jnp.einsum('bthd,chd->bthc', q_nope, w_uk)
    ckv = rms_norm(c_kv, kv_norm_g)
    kpe = rope(k_r, pos)
    mq = z[..., O_MQ:O_MK].reshape(B, T, ML_HEADS, ML_DH)
    mk = z[..., O_MK:O_MV].reshape(B, T, ML_HEADS, ML_DH) * (ML_DH ** -0.5)
    mv = z[..., O_MV:O_MO].reshape(B, T, ML_HEADS, ML_DH)
    og = jax.nn.sigmoid(z[..., O_MO:O_G])
    gates = z[..., O_G:].astype(jnp.float32) + b_gates.astype(jnp.float32)
    ig = gates[..., :ML_HEADS]
    lf = jax.nn.log_sigmoid(gates[..., ML_HEADS:])
    return q_lat, q_rope, ckv, kpe, mq, mk, mv, ig, lf, og

def mla_attend(q_lat, q_rope, q_pos, ckv, kpe, k_pos):
    s = jnp.einsum('bqhc,bkc->bhqk', q_lat, ckv) + jnp.einsum('bqhr,bkr->bhqk', q_rope, kpe)
    s = s.astype(jnp.float32) * SM_SCALE
    s = jnp.where(k_pos[None, :] <= q_pos[:, None], s, -jnp.inf)
    p = jax.nn.softmax(s, axis=-1).astype(ckv.dtype)
    return jnp.einsum('bhqk,bkc->bqhc', p, ckv)

def mla_prompt(q_lat, q_rope, ckv, kpe):
    B, T, H, C = q_lat.shape
    n_blk = -(-T // Q_BLOCK)
    pad = n_blk * Q_BLOCK - T
    qlb = jnp.pad(q_lat, ((0, 0), (0, pad), (0, 0), (0, 0))).reshape(B, n_blk, Q_BLOCK, H, C).transpose(1, 0, 2, 3, 4)
    qrb = jnp.pad(q_rope, ((0, 0), (0, pad), (0, 0), (0, 0))).reshape(B, n_blk, Q_BLOCK, H, QK_ROPE).transpose(1, 0, 2, 3, 4)
    pos_b = jnp.arange(n_blk * Q_BLOCK).reshape(n_blk, Q_BLOCK)
    k_pos = jnp.arange(T)
    out = lax.map(lambda a: mla_attend(a[0], a[1], a[2], ckv, kpe, k_pos), (qlb, qrb, pos_b))
    return out.transpose(1, 0, 2, 3, 4).reshape(B, n_blk * Q_BLOCK, H, C)[:, :T]

def mlstm_chunk(state, q, k, v, ig, lf):
    C0, n0, m0 = state
    q, k, v = (a.astype(jnp.float32) for a in (q, k, v))
    L = q.shape[1]
    b = jnp.cumsum(lf, axis=1).transpose(0, 2, 1)
    igh = ig.transpose(0, 2, 1)
    causal = jnp.tril(jnp.ones((L, L), dtype=bool))
    D = jnp.where(causal, b[..., :, None] - b[..., None, :] + igh[..., None, :], -jnp.inf)
    inter = b + m0[..., None]
    m = jnp.maximum(inter, D.max(-1))
    w = jnp.exp(D - m[..., None])
    a = jnp.exp(inter - m)
    wqk = w * jnp.einsum('blhd,bshd->bhls', q, k)
    num = a[..., None] * jnp.einsum('bhvk,blhk->bhlv', C0, q) + jnp.einsum('bhls,bshv->bhlv', wqk, v)
    den = a * jnp.einsum('bhk,blhk->bhl', n0, q) + wqk.sum(-1)
    h = num / jnp.maximum(jnp.abs(den), jnp.exp(-m))[..., None]
    bL = b[..., -1]
    dec = bL[..., None] - b + igh
    mL = jnp.maximum(bL + m0, dec.max(-1))
    ws = jnp.exp(dec - mL[..., None])
    aL = jnp.exp(bL + m0 - mL)
    CL = aL[..., None, None] * C0 + jnp.einsum('bhs,bshv,bshk->bhvk', ws, v, k)
    nL = aL[..., None] * n0 + jnp.einsum('bhs,bshk->bhk', ws, k)
    return (CL, nL, mL), h.transpose(0, 2, 1, 3)

def mlstm_prompt(q, k, v, ig, lf):
    B, T = q.shape[:2]
    f32 = jnp.float32
    state = (jnp.zeros((B, ML_HEADS, ML_DH, ML_DH), f32), jnp.zeros((B, ML_HEADS, ML_DH), f32),
             jnp.zeros((B, ML_HEADS), f32))
    state, h_meta = mlstm_chunk(state, q[:, :N_META], k[:, :N_META], v[:, :N_META], ig[:, :N_META], lf[:, :N_META])
    nc = (T - N_META) // CHUNK

    def split(a):
        a = a[:, N_META:]
        return a.reshape((B, nc, CHUNK) + a.shape[2:]).swapaxes(0, 1)

    state, h_rest = lax.scan(lambda s, xs: mlstm_chunk(s, *xs), state, tuple(split(a) for a in (q, k, v, ig, lf)))
    h_rest = h_rest.swapaxes(0, 1).reshape(B, nc * CHUNK, ML_HEADS, ML_DH)
    return state, jnp.concatenate([h_meta, h_rest], axis=1)

def mixer_output(o_lat, h_ml, og, w_kvb, mh_norm_g, w_o, dtype):
    B, T = o_lat.shape[:2]
    w_uv = w_kvb.reshape(KV_RANK, MLA_HEADS, QK_NOPE + V_DIM)[..., QK_NOPE:]
    o_mla = jnp.einsum('bthc,chv->bthv', o_lat, w_uv).reshape(B, T, MLA_W)
    mu = h_ml.mean(-1, keepdims=True)
    var = jnp.square(h_ml - mu).mean(-1, keepdims=True)
    hn = ((h_ml - mu) * lax.rsqrt(var + EPS)).reshape(B, T, ML_W)
    o_ml = (hn * mh_norm_g).astype(dtype) * og
    return jnp.einsum('bte,ed->btd', jnp.concatenate([o_mla.astype(dtype), o_ml], axis=-1), w_o)

def peer_block(x, w_pq, sub_keys, expert_u, expert_v):
    n = x.shape[0]
    q = jnp.einsum('nd,de->ne', x, w_pq).reshape(n, PEER_HEADS, 2, PEER_DQ // 2)
    s = jnp.einsum('nhpc,hpkc->nhpk', q, sub_keys).astype(jnp.float32)
    sv, si = lax.top_k(s, PEER_TOPK)
    cand = (sv[:, :, 0, :, None] + sv[:, :, 1, None, :]).reshape(n, PEER_HEADS, PEER_TOPK * PEER_TOPK)
    cv, ci = lax.top_k(cand, PEER_TOPK)
    e1 = jnp.take_along_axis(si[:, :, 0], ci // PEER_TOPK, axis=-1)
    e2 = jnp.take_along_axis(si[:, :, 1], ci % PEER_TOPK, axis=-1)
    experts = e1 * N_KEYS + e2
    g = jax.nn.softmax(cv, axis=-1)
    act = jax.nn.gelu(jnp.einsum('nhkd,nd->nhk', expert_u[experts], x).astype(jnp.float32))
    return jnp.einsum('nhk,nhkd->nd', (g * act).astype(x.dtype), expert_v[experts])

def peer(h, w_pq, sub_keys, expert_u, expert_v):
    shp = h.shape
    x = h.reshape(-1, D_MODEL)
    N = x.shape[0]
    nb = -(-N // PEER_BLOCK)
    xb = jnp.pad(x, ((0, nb * PEER_BLOCK - N), (0, 0))).reshape(nb, PEER_BLOCK, D_MODEL)
    out = lax.map(lambda xx: peer_block(xx, w_pq, sub_keys, expert_u, expert_v), xb)
    return out.reshape(-1, D_MODEL)[:N].reshape(shp)

def setup_inputs(seed: int = 0) -> dict:
    key = jax.random.key(seed)
    ks = jax.random.split(key, 32)
    nrm = jax.random.normal
    f32 = jnp.float32
    n_pages = PAST_LEN // PAGE_SIZE
    n_used = DEC_BATCH * n_pages
    n_pool = n_used + n_used // 4
    page_table = jax.random.permutation(ks[0], n_pool)[:n_used].reshape(DEC_BATCH, n_pages).astype(jnp.int32)

    def gain(k, shape):
        return 1.0 + 0.02 * nrm(k, shape, f32)

    b_gates = jnp.concatenate([0.1 * nrm(ks[1], (DEPTH, ML_HEADS), f32),
                               jnp.linspace(3.0, 6.0, ML_HEADS, dtype=f32)[None] + 0.1 * nrm(ks[2], (DEPTH, ML_HEADS), f32)], axis=-1)
    return {
        "x_prompt": nrm(ks[3], (BATCH, SEQ, D_MODEL), f32),
        "x_sample": nrm(ks[4], (DEC_BATCH, DEC_SEQ, D_MODEL), f32),
        "cache_ckv": nrm(ks[5], (DEPTH, n_pool, PAGE_SIZE, KV_RANK), f32),
        "cache_kpe": nrm(ks[6], (DEPTH, n_pool, PAGE_SIZE, QK_ROPE), f32),
        "page_table": page_table,
        "state_C": 0.1 * nrm(ks[7], (DEPTH, DEC_BATCH, ML_HEADS, ML_DH, ML_DH), f32),
        "state_n": 0.1 * nrm(ks[8], (DEPTH, DEC_BATCH, ML_HEADS, ML_DH), f32),
        "state_m": nrm(ks[9], (DEPTH, DEC_BATCH, ML_HEADS), f32),
        "meta_tokens": nrm(ks[10], (N_META, D_MODEL), f32),
        "ln_in_g": gain(ks[11], (D_MODEL,)),
        "ln_in_b": 0.02 * nrm(ks[12], (D_MODEL,), f32),
        "w_in": nrm(ks[13], (DEPTH, D_MODEL, IN_W), f32) * D_MODEL ** -0.5,
        "b_gates": b_gates,
        "q_norm_g": gain(ks[14], (DEPTH, Q_RANK)),
        "w_qb": nrm(ks[15], (DEPTH, Q_RANK, MLA_HEADS * (QK_NOPE + QK_ROPE)), f32) * Q_RANK ** -0.5,
        "kv_norm_g": gain(ks[16], (DEPTH, KV_RANK)),
        "w_kvb": nrm(ks[17], (DEPTH, KV_RANK, MLA_HEADS * (QK_NOPE + V_DIM)), f32) * KV_RANK ** -0.5,
        "mh_norm_g": gain(ks[18], (DEPTH, ML_W)),
        "w_o": nrm(ks[19], (DEPTH, MIX_W, D_MODEL), f32) * (MIX_W ** -0.5 * DN_BETA),
        "ln1_g": gain(ks[20], (DEPTH, D_MODEL)),
        "ln1_b": 0.02 * nrm(ks[21], (DEPTH, D_MODEL), f32),
        "w_pq": nrm(ks[22], (DEPTH, D_MODEL, PEER_HEADS * PEER_DQ), f32) * D_MODEL ** -0.5,
        "sub_keys": nrm(ks[23], (DEPTH, PEER_HEADS, 2, N_KEYS, PEER_DQ // 2), f32) * (PEER_DQ // 2) ** -0.5,
        "expert_u": nrm(ks[24], (DEPTH, N_EXPERTS, D_MODEL), f32) * D_MODEL ** -0.5,
        "expert_v": nrm(ks[25], (DEPTH, N_EXPERTS, D_MODEL), f32) * DN_BETA,
        "ln2_g": gain(ks[26], (DEPTH, D_MODEL)),
        "ln2_b": 0.02 * nrm(ks[27], (DEPTH, D_MODEL), f32),
    }

def reference(x_prompt, x_sample, cache_ckv, cache_kpe, page_table, state_C, state_n, state_m,
              meta_tokens, ln_in_g, ln_in_b, w_in, b_gates, q_norm_g, w_qb, kv_norm_g, w_kvb,
              mh_norm_g, w_o, ln1_g, ln1_b, w_pq, sub_keys, expert_u, expert_v, ln2_g, ln2_b):
    B = x_prompt.shape[0]
    DB, S = x_sample.shape[:2]
    dt = x_prompt.dtype
    meta = jnp.broadcast_to(meta_tokens[None].astype(dt), (B, N_META, D_MODEL))
    hp = layer_norm(jnp.concatenate([meta, x_prompt], axis=1), ln_in_g, ln_in_b)
    hs = layer_norm(x_sample, ln_in_g, ln_in_b)
    T = hp.shape[1]
    past_len = page_table.shape[1] * cache_ckv.shape[2]
    pos_p = jnp.arange(T)
    pos_s = past_len + jnp.arange(S)
    k_pos_s = jnp.arange(past_len + S)
    ckv_p_l, kpe_p_l, C_p_l, n_p_l, m_p_l = [], [], [], [], []
    ckv_s_l, kpe_s_l, C_s_l, n_s_l, m_s_l = [], [], [], [], []
    for l in range(DEPTH):
        q_lat, q_rope, ckv, kpe, mq, mk, mv, ig, lf, og = mixer_project(
            hp, pos_p, w_in[l], b_gates[l], q_norm_g[l], w_qb[l], kv_norm_g[l], w_kvb[l])
        o_lat = mla_prompt(q_lat, q_rope, ckv, kpe)
        (Cp, np_, mp), h_ml = mlstm_prompt(mq, mk, mv, ig, lf)
        a_p = mixer_output(o_lat, h_ml, og, w_kvb[l], mh_norm_g[l], w_o[l], dt)
        hp = layer_norm(DN_ALPHA * hp + a_p, ln1_g[l], ln1_b[l])
        hp = layer_norm(DN_ALPHA * hp + peer(hp, w_pq[l], sub_keys[l], expert_u[l], expert_v[l]), ln2_g[l], ln2_b[l])
        ckv_p_l.append(ckv); kpe_p_l.append(kpe)
        C_p_l.append(Cp.astype(dt)); n_p_l.append(np_.astype(dt)); m_p_l.append(mp.astype(dt))
        q_lat, q_rope, ckv, kpe, mq, mk, mv, ig, lf, og = mixer_project(
            hs, pos_s, w_in[l], b_gates[l], q_norm_g[l], w_qb[l], kv_norm_g[l], w_kvb[l])
        ckv_all = jnp.concatenate([cache_ckv[l][page_table].reshape(DB, past_len, KV_RANK).astype(ckv.dtype), ckv], axis=1)
        kpe_all = jnp.concatenate([cache_kpe[l][page_table].reshape(DB, past_len, QK_ROPE).astype(kpe.dtype), kpe], axis=1)
        o_lat = mla_attend(q_lat, q_rope, pos_s, ckv_all, kpe_all, k_pos_s)
        st = (state_C[l].astype(jnp.float32), state_n[l].astype(jnp.float32), state_m[l].astype(jnp.float32))
        (Cs, ns, ms), h_ml = mlstm_chunk(st, mq, mk, mv, ig, lf)
        a_s = mixer_output(o_lat, h_ml, og, w_kvb[l], mh_norm_g[l], w_o[l], dt)
        hs = layer_norm(DN_ALPHA * hs + a_s, ln1_g[l], ln1_b[l])
        hs = layer_norm(DN_ALPHA * hs + peer(hs, w_pq[l], sub_keys[l], expert_u[l], expert_v[l]), ln2_g[l], ln2_b[l])
        ckv_s_l.append(ckv); kpe_s_l.append(kpe)
        C_s_l.append(Cs.astype(dt)); n_s_l.append(ns.astype(dt)); m_s_l.append(ms.astype(dt))
    y_prompt = hp[:, N_META:]
    y_sample = hs
    return (y_prompt, y_sample,
            jnp.stack(ckv_p_l), jnp.stack(kpe_p_l), jnp.stack(C_p_l), jnp.stack(n_p_l), jnp.stack(m_p_l),
            jnp.stack(ckv_s_l), jnp.stack(kpe_s_l), jnp.stack(C_s_l), jnp.stack(n_s_l), jnp.stack(m_s_l))


_drawn_inputs = setup_inputs


def setup_inputs(seed=0):
    import zlib

    import numpy as np

    out = dict(_drawn_inputs(seed))
    spreads = {}
    factors = {'q_norm_g': 7.058, 'kv_norm_g': 2.749, 'mh_norm_g': 3.405, 'ln2_g': 2.788, 'ln2_b': 3.118}
    for name, (base, spread) in spreads.items():
        noise = np.random.default_rng([zlib.crc32(name.encode()), seed]).standard_normal(out[name].shape)
        drawn = base * np.exp(spread * noise) if base else spread * noise
        out[name] = __import__('jax').numpy.asarray(drawn.astype(out[name].dtype))
    for name, factor in factors.items():
        out[name] = (out[name] * factor).astype(out[name].dtype)
    return out
```

```python
from contextlib import ExitStack

import concourse.bass as bass
from concourse import mybir

ALU = mybir.AluOpType
ACT = mybir.ActivationFunctionType
F32 = mybir.dt.float32
I32 = mybir.dt.int32
U32 = mybir.dt.uint32
AX = mybir.AxisListType.X

D = 1024
KD = D // 128
NS = 32
SB, SS = 8, 4
NPR = 528
NT = NS + NPR
TR = 112
TI = NT // TR
HALF = NT // 2
NH, NOPE, ROPE, VD = 8, 64, 32, 64
MH, DH = 4, 128
QR, KVR = 256, 128
SM_SCALE = float((NOPE + ROPE) ** -0.5)
PAGES, PAGE = 16, 128
PH, NK, TOPK = 8, 128, 16
ALPHA = float(2.0 ** 0.25)
BIG = 1e30
GT = 4
NG = HALF // GT
Z0W = QR + KVR + ROPE + 2 * MH

CONSTS = dict(ident=128, iota=128, ones=128, mask=TI * NT, ltd0=TR, ltdc=TR, lt01=TR, smask=SB * NS, sellast=128,
              lsel=NS, selb=SB, lastb=SB, pmask=1, cos=TI * 16, sin=TI * 16)
VECS = dict(qg=QR, kvg=KVR, mhg=MH * DH, bg=2 * MH, m0=TI * MH)


def offsets(table, at=0):
    out = {}
    for name, n in table.items():
        out[name] = (at, n)
        at += n
    return out, at


CO, C_END = offsets(CONSTS)
VO, V_END = offsets(VECS, C_END)
SMALL = V_END
XT0 = 5504
BODY = XT0 + KD * NT


def build(nc, x, consts, vecs, lnin, ln1, ln2, w_in, w_qb, w_uk, w_uv, w_o, w_pq, sub_keys,
          eu, ev, cache_t, cache_n, cache_r, pages, ct0, nt0,
          o_y, o_ckv, o_kpe, o_c, o_n, o_m, o_cs, o_ns):
    with ExitStack() as ctx:
        arena = ctx.enter_context(nc.sbuf_tensor("arena", [128, 52900], F32))
        ps = ctx.enter_context(nc.psum_tensor("ps", [128, 8, 512], F32))
        ptab = ctx.enter_context(nc.sbuf_tensor("ptab", [1, SB * PAGES], I32))

        def sem(name):
            return ctx.enter_context(nc.semaphore(name))

        def view(off, *dims, rows=128, r0=0):
            n = 1
            for d in dims:
                n *= d
            a = arena[r0:r0 + rows, off:off + n]
            if len(dims) == 1:
                return a
            if len(dims) == 2:
                return a.rearrange("p (a b) -> p a b", a=dims[0])
            if len(dims) == 3:
                return a.rearrange("p (a b c) -> p a b c", a=dims[0], b=dims[1])
            return a.rearrange("p (a b c d) -> p a b c d", a=dims[0], b=dims[1], c=dims[2])

        def const(name, *dims, rows=128):
            off, n = (CO | VO)[name]
            return view(off, *(dims or (n,)), rows=rows)

        ident, iota, ones = const("ident"), const("iota"), const("ones")
        mask = const("mask", TI, NT, rows=TR)
        smask = const("smask", SB, NS, rows=NS)
        cos, sin = const("cos", TI, 16, rows=TR), const("sin", TI, 16, rows=TR)

        small_at = [SMALL]

        def small(*dims, rows=TR):
            n = 1
            for d in dims:
                n *= d
            v = view(small_at[0], *dims, rows=rows)
            small_at[0] += n
            assert small_at[0] <= XT0
            return v

        st6 = small(MH, 6)
        mv2 = small(2)
        mvh = small(MH, 2)
        rstd = small(TI)
        rs1, rs4 = small(1), small(MH)
        gat = small(TI, 2 * MH)
        gabs, glog = small(TI, MH), small(TI, MH)
        lf, cum, cs = small(TI, MH), small(TI, MH), small(TI, MH)
        mm, mabs, nm = small(TI, MH), small(TI, MH), small(TI, MH)
        emm, am = small(TI, MH), small(TI, MH)
        den, rden = small(MH), small(MH)
        mx1, nb, rsum, rrec = small(2, 1), small(2, 1), small(2, 1), small(2, 1)
        nml = small(MH, rows=128)
        wsp = small(TI, MH)
        nq = small(MH, SB, rows=NS)
        ssq = small(TI, 2)
        mx4 = small(MH)
        wss = small(MH, rows=NS)
        smx = small(4, rows=NS)
        nqs = small(MH, rows=NS)
        mlast = small(MH, rows=NS)

        hT = view(XT0, KD, NT)
        cs_bc = view(XT0, MH, NT)
        wexp = view(XT0 + MH * NT, MH, NT, rows=TR)
        H0 = BODY
        hid = view(H0, TI, D, rows=TR)
        LNV = H0 + TI * D
        lnv = view(LNV, 2, D, rows=TR)
        TT0 = LNV + 2 * D
        tt = view(TT0, 8, NT)
        MQ0 = TT0 + 8 * NT
        mqT = view(MQ0, MH, NT)
        Z0 = MQ0 + MH * NT
        z0 = view(Z0, TI, Z0W, rows=TR)
        ZK = Z0 + TI * Z0W
        zkvo = view(ZK, 3, TI, 512, rows=TR)
        zk, zv, zo = zkvo[:, 0], zkvo[:, 1], zkvo[:, 2]
        W0 = ZK + 3 * TI * 512
        wring = view(W0, 2, KD, 512)
        olT = view(W0, NH, NT)
        WQB = W0 + NH * NT
        wqb = view(WQB, 2, NH * (NOPE + ROPE))
        Q0 = W0 + 2 * KD * 512
        qnT = view(Q0, 4, NT)
        sbuf_s = view(Q0, 2, NT, rows=TR)
        sbuf_pt = view(Q0 + 2 * NT, 2, NT, rows=TR)
        QRT = Q0 + 4 * NT
        qrT = view(QRT, 2, NT)
        QRK = QRT + 2 * NT
        qrk = view(QRK, TI, NH * ROPE, rows=TR)
        QL = QRK + TI * NH * ROPE
        qlT = view(QL, NH, NT)
        kp4 = view(QL, TI, 4, ROPE, rows=TR)
        junk = view(QL + 640, D, rows=TR)
        rtmp = view(QL + 1664, 4, TI * 16, rows=TR)
        WUK = 51876
        wuk, wuv = view(WUK, 4, 128), view(WUK + 512, NH * VD)
        ct = view(QL, MH * SB, DH)
        cach_n = [view(Q0 + p * 4608, PAGES, KVR) for p in range(2)]
        cach_t = [view(Q0 + p * 4608 + 2048, PAGES * PAGE) for p in range(2)]
        cach_r = [view(Q0 + p * 4608 + 4096, 512) for p in range(2)]
        qs = view(LNV, SB, NH * SS)
        qrs4 = view(LNV + 256, SB, NH * SS)
        qrc = view(LNV + 512, NH, 4, ROPE, rows=NS)
        nst = view(LNV + 1536, MH, SB)
        numT = view(LNV + 1568, MH, NS)
        numi = view(QRK, MH, DH, rows=NS)
        hbuf = view(QRK + 512, MH, DH, rows=TR)
        rqt = view(LNV, 4, NH, 16, rows=TR)
        dg = view(XT0 + MH * NT, 2, MH, TR, rows=TR)
        vw = view(Q0, 2, MH * DH, rows=TR)
        cst = view(Q0 + 2 * NT, MH * DH + MH)
        sR = view(Q0 + 1700, MH, SB, rows=NS)
        aLb = view(Q0 + 1732, MH * SB)
        wsb = view(Q0 + 1764, MH, SB, rows=NS)
        s_p = view(XT0, PAGES * PAGE + NS, rows=NS)
        s_pt = view(XT0 + 2080, PAGES + 1, NS)
        s_mx = view(XT0 + 2080 + 544, 4, rows=NS)
        XM = Q0
        xm = view(XM, KD, NT)
        WO = MQ0
        wo = view(WO, KD, D)
        SK = XM + KD * NT
        skT = view(SK, 16, NK)
        pqT = view(SK + 2048, 2, NT)
        wpq = [view(W0 + p * 4096, KD, 512) for p in range(2)]
        sc = view(H0, TI, 16, NK, rows=TR)
        TK = MQ0
        sv = view(TK, 16, TOPK, rows=TR)
        siu = view(TK + 256, 16, TOPK, rows=TR).bitcast(U32)
        sif = view(TK + 512, 16, TOPK, rows=TR)
        tks = view(TK + 768, 256, rows=TR)
        cand = view(TK + 1024, 256, rows=TR)
        cv = view(TK + 1280, PH, TOPK, rows=TR)
        ciu = view(TK + 1408, PH, TOPK, rows=TR).bitcast(U32)
        ca = view(TK + 1536, 2, PH * TOPK, rows=TR)
        cau = view(TK + 1792, 2, PH * TOPK, rows=TR).bitcast(U32)
        pick = view(TK + 2048, 3, PH * TOPK, rows=TR)
        eq = view(TK + 2560, PH, TOPK, TOPK, rows=TR)
        tsum = view(TK + 4608, PH, rows=TR)
        P0 = CO["mask"][0]
        pickT = view(P0, 3, NT)
        ab = view(P0 + 3 * NT, 2, HALF)
        hb = view(P0 + 3 * NT + 2 * HALF, 2, HALF)
        G0 = BODY
        gm = view(G0, HALF, NK)
        UV = G0 + HALF * NK
        ut = [view(UV + p * 2048, KD, 128) for p in range(2)]
        vt = [view(UV + p * 2048 + 1024, D) for p in range(2)]
        oh = [view(UV + 4096 + p * 1024, 2, GT, NK) for p in range(2)]
        pk4 = [view(UV + 6144 + p * 12, 3, GT) for p in range(2)]
        assert UV + 6168 <= 52900
        yt = view(G0, TI, D, rows=TR)
        lnv2 = view(G0 + TI * D, 2, D, rows=TR)

        s = {n: sem(n) for n in (
            "x_in consts_in ln_in w_in0 w_in1 wq_in uk_in ct_in nst_in dve_step act_step "
            "var_ready std_ready ln_done ht_ps ht_done z_ps z_done ssq_ready rms_std "
            "tok_done tt_ps tt_done q_ps q_done rot_done qrt_ps qrt_done qrc_ready qrs_ps qs_ready "
            "ls_abs ls_log lf_ready cum_ps dg_ready dg_ps csbc_done "
            "mla_s mla_max mla_exp mla_p mla_tps mla_pt mla_o mla_done "
            "inter_ps numt_done numi_ps inter_done ml_m ml_w ml_qk ml_p ml_tps ml_pt ml_num ml_h hvar hstd ml_gated "
            "mlast_ps ws_lin ws_exp wsp_done vw_ready cst_ps cst_done sel_ready sel_ps sws_lin sws_exp wsb_done "
            "vwb_ready sst_ps sst_done c_in0 c_in1 sm_s sm_max sm_exp sm_p sm_tps sm_pt sm_o sm_done "
            "wo_in ln1_in xm_ps xm_done wo_ps res_done pq_in0 pq_in1 sk_in pq_ps pq_done sc_ps sc_done "
            "tk_lin tk_exp tk_pick pk_ps pk_done oh_ready g_ps g_done u_in0 u_in1 v_in0 v_in1 "
            "s_ps a_done h_done y_ps y_done ln2_in yt_ps yt_done pt_in pk4_done "
            "out_tok out_m out_c out_cs out_y").split()}
        w_in_sem, c_in, pq_in, u_in, v_in = ([a, b] for a, b in (
            (s["w_in0"], s["w_in1"]), (s["c_in0"], s["c_in1"]), (s["pq_in0"], s["pq_in1"]), (s["u_in0"], s["u_in1"]), (s["v_in0"], s["v_in1"])))
        PIECES = [(d, 0, HALF, d, 0) for d in range(6)] + [(6, 0, 232, 0, HALF), (7, 0, 232, 1, HALF),
                                                           (6, 232, 48, 2, HALF), (7, 232, 48, 2, HALF + 48)]
        NJ = TI * NH

        def tile(i):
            return slice(i * TR, (i + 1) * TR)

        def half(n):
            return slice(n * HALF, (n + 1) * HALF)

        def bc(ap, axis, n):
            return ap.unsqueeze(axis).broadcast_to(ap.shape[:axis] + [n] + ap.shape[axis:]) if isinstance(ap.shape, list) \
                else ap.unsqueeze(axis).broadcast_to(list(ap.shape[:axis]) + [n] + list(ap.shape[axis:]))

        block = ctx.enter_context(nc.Block())

        @block.sync
        def _(sp):
            sp.dma_start(ptab[:, :], pages).then_inc(s["pt_in"], 16)
            sp.dma_start(hid, x.rearrange("(i p) d -> p i d", p=TR)).then_inc(s["x_in"], 16)
            sp.dma_start(lnv, lnin[0:TR]).then_inc(s["ln_in"], 16)
            sp.dma_start(arena[:, 0:C_END], consts).then_inc(s["consts_in"], 16)
            sp.dma_start(arena[:, C_END:V_END], vecs).then_inc(s["consts_in"], 16)
            for c in range(5):
                if c >= 2:
                    sp.wait_ge(s["z_ps"], TI * (c - 1))
                sp.dma_start(wring[:, c % 2], w_in[c]).then_inc(w_in_sem[c % 2], 16)
            sp.dma_start(wuk, w_uk).then_inc(s["uk_in"], 16)
            sp.dma_start(wuv, w_uv).then_inc(s["uk_in"], 16)
            sp.wait_ge(s["z_ps"], 4 * TI)
            sp.dma_start(wqb, w_qb).then_inc(s["wq_in"], 16)
            sp.wait_ge(s["tok_done"], 1)
            sp.dma_start(o_ckv.rearrange("(i p) c -> p i c", p=TR), z0[:, :, QR:QR + KVR]).then_inc(s["out_tok"], 16)
            sp.dma_start(o_kpe.rearrange("(i p) c -> p i c", p=TR),
                         z0[:, :, QR + KVR:QR + KVR + ROPE]).then_inc(s["out_tok"], 16)
            sp.wait_ge(s["qs_ready"], 1)
            sp.dma_start(nst, nt0).then_inc(s["nst_in"], 16)
            sp.wait_ge(s["mla_s"], NJ)
            sp.dma_start(ct, ct0).then_inc(s["ct_in"], 16)
            sp.wait_ge(s["cst_done"], 1)
            sp.dma_start(o_c, cst[:, 0:512]).then_inc(s["out_c"], 16)
            sp.dma_start(o_n, cst[:, 512:516]).then_inc(s["out_c"], 16)
            sp.dma_start(o_m.rearrange("(i p) h -> p i h", p=TR), mabs).then_inc(s["out_m"], 16)
            sp.wait_ge(s["sst_done"], SB + 1)
            sp.dma_start(o_cs, ct).then_inc(s["out_cs"], 16)
            sp.dma_start(o_ns, nst).then_inc(s["out_cs"], 16)
            sp.wait_ge(s["out_c"], 32)
            sp.wait_ge(s["out_cs"], 32)
            sp.wait_ge(s["pt_in"], 16)
            for b in range(SB):
                p = b % 2
                if b >= 2:
                    sp.wait_ge(s["sm_o"], b - 1)
                with sp.Fori(0, PAGES // 4) as kq:
                    for r in range(4):
                        page = sp.value_load(ptab[0:1, bass.ds(kq * 4 + (b * PAGES + r), 1)], min_val=0, max_val=cache_t.shape[0] - 1)
                        sp.dma_start(cach_t[p][:, bass.ds(kq * 512 + r * 128, 128)],
                                     cache_t[bass.ds(page, 1)].rearrange("a c k -> (a c) k")).then_inc(c_in[p], 16)
                        sp.dma_start(cach_n[p][:, bass.ds(kq * 4 + r, 1), :].rearrange("p a c -> p (a c)"),
                                     cache_n[bass.ds(page, 1)].rearrange("a k c -> (a k) c")).then_inc(c_in[p], 16)
                for k in range(PAGES):
                    page = sp.value_load(ptab[0:1, b * PAGES + k:b * PAGES + k + 1], min_val=0, max_val=cache_t.shape[0] - 1)
                    q = k // 4
                    sp.dma_start(cach_r[p][32 * q:32 * q + 32, (k % 4) * 128:(k % 4) * 128 + 128],
                                 cache_r[bass.ds(page, 1)].rearrange("a r k -> (a r) k")).then_inc(c_in[p], 16)
            sp.wait_ge(s["sm_done"], SB)
            sp.wait_ge(s["out_tok"], 32)
            sp.dma_start(wo, w_o).then_inc(s["wo_in"], 16)
            sp.dma_start(lnv, ln1[0:TR]).then_inc(s["ln1_in"], 16)
            sp.dma_start(skT, sub_keys).then_inc(s["sk_in"], 16)
            sp.wait_ge(s["xm_done"], 13)
            for c in range(4):
                if c >= 2:
                    sp.wait_ge(s["sc_ps"], 4 * (c - 1))
                sp.dma_start(wpq[c % 2], w_pq[c]).then_inc(pq_in[c % 2], 16)

            def expert_block(p, blk, n):
                if n is not None:
                    sp.wait_ge(s["s_ps"], n)
                sp.dma_start(ut[p], eu[blk]).then_inc(u_in[p], 16)
                if n is not None:
                    sp.wait_ge(s["y_ps"], n)
                sp.dma_start(vt[p], ev[blk]).then_inc(v_in[p], 16)

            sp.wait_ge(s["sc_ps"], 16)
            sp.wait_ge(s["sc_done"], 16)
            expert_block(0, 0, None)
            expert_block(1, 1, None)
            with sp.Fori(1, NK // 2) as j:
                for p in range(2):
                    expert_block(p, j * 2 + p, j * 2 + (p - 1))
            for p in range(2):
                expert_block(p, p, NK + p - 1)
            with sp.Fori(1, NK // 2) as j:
                for p in range(2):
                    expert_block(p, j * 2 + p, j * 2 + (NK + p - 1))
            sp.wait_ge(s["h_done"], 2 * NK)
            sp.dma_start(lnv2, ln2[0:TR]).then_inc(s["ln2_in"], 16)
            for i in range(TI):
                sp.wait_ge(s["ln_done"], 2 * TI + i + 1)
                sp.dma_start(o_y[tile(i), :], yt[:, i, :]).then_inc(s["out_y"], 16)
            sp.wait_ge(s["out_m"], 16)
            sp.wait_ge(s["out_y"], 16 * TI)

        @block.tensor
        def _(pe):
            pe.wait_ge(s["consts_in"], 32)

            def hidden_transposes(n):
                i = n % TI
                pe.wait_ge(s["ln_done"], n + 1)
                if n >= 2:
                    pe.wait_ge(s["ht_done"], n - 1)
                for k in range(KD):
                    last = nc.tensor.transpose(ps[:, 4 + 2 * (n % 2) + k // 4, (k % 4) * TR:(k % 4 + 1) * TR],
                                               hid[:, i, k * 128:(k + 1) * 128], ident[0:TR, 0:TR])
                last.then_inc(s["ht_ps"], 1)

            for i in range(TI):
                hidden_transposes(i)
            for g in range(4 * TI + 2 * MH):
                c, i = (g // TI, g % TI) if g < 4 * TI else (4, TI - 1)
                if i == 0 or g == 4 * TI:
                    pe.wait_ge(w_in_sem[c % 2], 16 * (c // 2 + 1))
                pe.wait_ge(s["ht_done"], i + 1)
                if g >= 4:
                    pe.wait_ge(s["z_done"], g - 3)
                for k in range(KD):
                    if c == 0:
                        last = nc.tensor.matmul(ps[0:TR, g % 4, 0:Z0W], hT[:, k, tile(i)], wring[:, 0, k, 0:Z0W],
                                                start=(k == 0), stop=(k == KD - 1))
                    elif c < 4:
                        last = nc.tensor.matmul(ps[0:TR, g % 4, :], hT[:, k, tile(i)], wring[:, c % 2, k, :],
                                                start=(k == 0), stop=(k == KD - 1))
                    else:
                        h, n = (g - 4 * TI) // 2, g % 2
                        last = nc.tensor.matmul(ps[:, g % 4, 0:HALF], wring[:, 0, k, h * 128:(h + 1) * 128],
                                                hT[:, k, half(n)], start=(k == 0), stop=(k == KD - 1))
                last.then_inc(s["z_ps"], 1)
            pe.wait_ge(s["tok_done"], 1)
            pe.wait_ge(s["ht_done"], TI)
            for i in range(TI):
                if i >= 2:
                    pe.wait_ge(s["tt_done"], i - 1)
                a, b = 4 + 2 * (i % 2), 5 + 2 * (i % 2)
                srcs = [z0[:, i, QR:QR + KVR], kp4[:, i].rearrange("p a r -> p (a r)"), z0[:, i, 0:128], z0[:, i, 128:256]]
                for n, src in enumerate(srcs):
                    nc.tensor.transpose(ps[:, a, n * TR:(n + 1) * TR], src, ident[0:TR, 0:TR])
                for h in range(MH):
                    last = nc.tensor.transpose(ps[:, b, h * TR:(h + 1) * TR], zk[:, i, h * 128:(h + 1) * 128],
                                               ident[0:TR, 0:TR])
                last.then_inc(s["tt_ps"], 1)
            pe.wait_ge(s["wq_in"], 16)
            pe.wait_ge(s["uk_in"], 32)
            pe.wait_ge(s["tt_done"], TI)
            pe.wait_ge(s["z_done"], 28)
            for g in range(29):
                if g >= 4:
                    pe.wait_ge(s["q_done"], g - 3)
                if g < 8:
                    for k in range(2):
                        last = nc.tensor.matmul(ps[:, g % 4, 0:HALF], wqb[:, k, (g // 2) * 128:(g // 2 + 1) * 128],
                                                tt[:, 2 + k, half(g % 2)], start=(k == 0), stop=(k == 1))
                elif g < 13:
                    for k in range(2):
                        last = nc.tensor.matmul(ps[0:TR, g % 4, 0:NH * ROPE], tt[:, 2 + k, tile(g - 8)],
                                                wqb[:, k, 512:768], start=(k == 0), stop=(k == 1))
                else:
                    h, n = (g - 13) // 2, (g - 13) % 2
                    o = 64 * (h % 2)
                    last = nc.tensor.matmul(ps[:, g % 4, 0:HALF], wuk[o:o + 64, h // 2, :], qnT[o:o + 64, h // 2, half(n)],
                                            start=True, stop=True)
                last.then_inc(s["q_ps"], 1)
            for i in range(TI):
                pe.wait_ge(s["rot_done"], i + 1)
                if i >= 2:
                    pe.wait_ge(s["qrt_done"], i - 1)
                for n in range(2):
                    last = nc.tensor.transpose(ps[:, 4 + i % 2, n * TR:(n + 1) * TR], qrk[:, i, n * 128:(n + 1) * 128],
                                               ident[0:TR, 0:TR])
                last.then_inc(s["qrt_ps"], 1)
            pe.wait_ge(s["qrc_ready"], 1)
            for h in range(NH):
                last = nc.tensor.transpose(ps[:, 6, h * NS:(h + 1) * NS], qrc[:, h].rearrange("p a r -> p (a r)"),
                                           ident[0:NS, 0:NS])
            last.then_inc(s["qrs_ps"], 1)
            pe.wait_ge(s["lf_ready"], 1)
            for t in range(TI):
                for u in range(t + 1):
                    m = const("ltd0" if t == 0 else "ltdc", rows=TR) if u == t else \
                        const("lt01", rows=TR) if u == 0 else ones[0:TR, 0:TR]
                    last = nc.tensor.matmul(ps[0:TR, 7, t * MH:(t + 1) * MH], m, lf[:, u, :], start=(u == 0), stop=(u == t))
            last.then_inc(s["cum_ps"], 1)
            for i in range(TI):
                pe.wait_ge(s["dg_ready"], i + 1)
                if i == 0:
                    pe.wait_ge(s["qrt_done"], TI)
                if i >= 2:
                    pe.wait_ge(s["csbc_done"], i - 1)
                nc.tensor.matmul(ps[:, 4 + i % 2, 0:MH * TR], ones[0:TR, :], dg[:, i % 2].rearrange("p h t -> p (h t)"),
                                 start=True, stop=True).then_inc(s["dg_ps"], 1)
            pe.wait_ge(s["q_done"], 29)
            pe.wait_ge(s["csbc_done"], TI)
            pe.wait_ge(s["qs_ready"], 1)

            def mla_scores(j):
                i, h = divmod(j, NH)
                if j >= 2:
                    pe.wait_ge(s["mla_max"], j - 1)
                o = 32 * (h % 4)
                nk = TR * (i + 1)
                for lo, hi in ((0, min(nk, 512)),) + (((512, nk),) if nk > 512 else ()):
                    out = ps[0:TR, 2 * (j % 2) + lo // 512, 0:hi - lo]
                    nc.tensor.matmul(out, qlT[:, h, tile(i)], tt[:, 0, lo:hi], start=True, stop=False)
                    last = nc.tensor.matmul(out, qrT[o:o + 32, h // 4, tile(i)], tt[o:o + 32, 1, lo:hi],
                                            start=False, stop=True, tile_position=(o, 0))
                last.then_inc(s["mla_s"], 1)

            def turn(src, i):
                for t in range(i + 1):
                    last = nc.tensor.transpose(ps[0:TR, 4 + t // 4, (t % 4) * TR:(t % 4 + 1) * TR], src[:, tile(t)],
                                               ident[0:TR, 0:TR])
                return last

            def mla_turn(j):
                pe.wait_ge(s["mla_p"], j + 1)
                if j >= 1:
                    pe.wait_ge(s["mla_pt"], j)
                turn(sbuf_s[:, j % 2], j // NH).then_inc(s["mla_tps"], 1)

            def mla_values(j):
                i = j // NH
                pe.wait_ge(s["mla_pt"], j + 1)
                if j >= 2:
                    pe.wait_ge(s["mla_done"], j - 1)
                for t in range(i + 1):
                    last = nc.tensor.matmul(ps[:, 6 + j % 2, 0:TR], z0[:, t, QR:QR + KVR], sbuf_pt[:, j % 2, tile(t)],
                                            start=(t == 0), stop=(t == i))
                last.then_inc(s["mla_o"], 1)

            for j in range(NJ + 2):
                if j < NJ:
                    mla_scores(j)
                if 1 <= j <= NJ:
                    mla_turn(j - 1)
                if j >= 2:
                    mla_values(j - 2)
            pe.wait_ge(s["ct_in"], 16)
            pe.wait_ge(s["nst_in"], 16)
            pe.wait_ge(s["mla_done"], NJ)
            for h in range(MH):
                for b in range(SB):
                    nc.tensor.matmul(ps[:, 6, h * NS + 4 * b:h * NS + 4 * b + 4], ct[:, h * SB + b, :],
                                     mqT[:, h, 4 * b:4 * b + 4], start=True, stop=True)
            for h in range(MH):
                last = nc.tensor.matmul(ps[0:NS, 6, 256 + h * SB:256 + (h + 1) * SB], mqT[:, h, 0:NS], nst[:, h, :],
                                        start=True, stop=True)
            last.then_inc(s["inter_ps"], 1)
            pe.wait_ge(s["numt_done"], 1)
            for h in range(MH):
                last = nc.tensor.transpose(ps[0:NS, 7, h * 128:(h + 1) * 128], numT[:, h, :], ident)
            last.then_inc(s["numi_ps"], 1)
            pe.wait_ge(s["inter_done"], 1)

            def ml_scores(n):
                i, h = divmod(n, MH)
                if n >= 2:
                    pe.wait_ge(s["ml_p"], n - 1)
                nk = TR * (i + 1)
                for lo, hi in ((0, min(nk, 512)),) + (((512, nk),) if nk > 512 else ()):
                    last = nc.tensor.matmul(ps[0:TR, 2 * (n % 2) + lo // 512, 0:hi - lo], mqT[:, h, tile(i)],
                                            tt[:, 4 + h, lo:hi], start=True, stop=True)
                last.then_inc(s["ml_qk"], 1)

            def ml_turn(n):
                i, h = divmod(n, MH)
                pe.wait_ge(s["ml_p"], n + 1)
                if n >= 1:
                    pe.wait_ge(s["ml_pt"], n)
                turn(wexp[:, h], i).then_inc(s["ml_tps"], 1)

            def ml_values(n):
                i, h = divmod(n, MH)
                pe.wait_ge(s["ml_pt"], n + 1)
                if i >= 1 and h == 0:
                    pe.wait_ge(s["ml_h"], i)
                for t in range(i + 1):
                    last = nc.tensor.matmul(ps[0:TR, 6, h * 128:(h + 1) * 128], sbuf_pt[:, n % 2, tile(t)],
                                            zv[:, t, h * 128:(h + 1) * 128], start=(t == 0), stop=(t == i))
                last.then_inc(s["ml_num"], 1)

            for i in range(TI):
                for h in range(MH + 2):
                    n = i * MH + h
                    if h < MH:
                        ml_scores(n)
                    if 1 <= h <= MH:
                        ml_turn(n - 1)
                    if h >= 2:
                        ml_values(n - 2)
            nc.tensor.matmul(ps[:, 7, 0:MH], const("sellast", rows=TR), mm[:, TI - 1, :], start=True, stop=True)
            nc.tensor.matmul(ps[0:NS, 7, 8:8 + MH], const("lsel", rows=NS), mm[0:NS, 0, :],
                             start=True, stop=True).then_inc(s["mlast_ps"], 1)
            pe.wait_ge(s["wsp_done"], 1)
            for i in range(TI):
                pe.wait_ge(s["vw_ready"], i + 1)
                for h in range(MH):
                    k = zk[:, i, h * 128:(h + 1) * 128]
                    nc.tensor.matmul(ps[:, 0, h * 128:(h + 1) * 128], k, vw[:, i % 2, h * 128:(h + 1) * 128],
                                     start=(i == 0 and h == 0), stop=(i == TI - 1), skip_group_check=True)
                    last = nc.tensor.matmul(ps[:, 1, h:h + 1], k, wsp[:, i, h:h + 1],
                                            start=(i == 0 and h == 0), stop=(i == TI - 1), skip_group_check=True)
                last.then_inc(s["cst_ps"], 1)
            pe.wait_ge(s["sel_ready"], 1)
            nc.tensor.matmul(ps[:, 7, 16:48], ones[0:NS, :], sR.rearrange("p h b -> p (h b)"),
                             start=True, stop=True).then_inc(s["sel_ps"], 1)
            pe.wait_ge(s["wsb_done"], 1)
            for h in range(MH):
                last = nc.tensor.matmul(ps[:, 6, h * SB:(h + 1) * SB], zk[0:NS, 0, h * 128:(h + 1) * 128], wsb[:, h, :],
                                        start=True, stop=True)
            last.then_inc(s["sst_ps"], 1)
            for b in range(SB):
                pe.wait_ge(s["vwb_ready"], b + 1)
                if b >= 2:
                    pe.wait_ge(s["sst_done"], b)
                for h in range(MH):
                    last = nc.tensor.matmul(ps[:, 2 + b % 2, h * 128:(h + 1) * 128], zk[0:NS, 0, h * 128:(h + 1) * 128],
                                            vw[0:NS, b % 2, h * 128:(h + 1) * 128], start=True, stop=True)
                last.then_inc(s["sst_ps"], 1)
            pe.wait_ge(s["sst_done"], SB + 1)
            pe.wait_ge(s["cst_done"], 1)
            for b in range(SB):
                p = b % 2
                pe.wait_ge(c_in[p], 16 * 3 * PAGES * (b // 2 + 1))
                if b >= 1:
                    pe.wait_ge(s["sm_max"], b)
                    pe.wait_ge(s["sm_exp"], b)
                for q in range(4):
                    nc.tensor.matmul(ps[0:NS, q, :], qs[:, b, :], cach_t[p][:, q * 512:(q + 1) * 512], start=True, stop=False)
                    nc.tensor.matmul(ps[0:NS, q, :], qrs4[32 * q:32 * q + 32, b, :], cach_r[p][32 * q:32 * q + 32, :],
                                     start=False, stop=True, tile_position=(32 * q, 0))
                nc.tensor.matmul(ps[0:NS, 4, 0:NS], qs[:, b, :], tt[:, 0, 0:NS], start=True, stop=False)
                nc.tensor.matmul(ps[0:NS, 4, 0:NS], qrs4[0:32, b, :], tt[0:32, 1, 0:NS],
                                 start=False, stop=True, tile_position=(0, 0)).then_inc(s["sm_s"], 1)
                pe.wait_ge(s["sm_p"], b + 1)
                for k in range(PAGES):
                    nc.tensor.transpose(ps[:, 5, k * NS:(k + 1) * NS], s_p[:, k * 128:(k + 1) * 128], ident[0:NS, 0:NS])
                nc.tensor.transpose(ps[0:NS, 6, 0:NS], s_p[:, 2048:2048 + NS], ident[0:NS, 0:NS]).then_inc(s["sm_tps"], 1)
                pe.wait_ge(s["sm_pt"], b + 1)
                if b >= 1:
                    pe.wait_ge(s["sm_done"], b)
                for k in range(PAGES):
                    nc.tensor.matmul(ps[:, 7, 0:NS], cach_n[p][:, k, :], s_pt[:, k, :], start=(k == 0), stop=False)
                nc.tensor.matmul(ps[:, 7, 0:NS], z0[0:NS, 0, QR:QR + KVR], s_pt[0:NS, PAGES, :],
                                 start=False, stop=True).then_inc(s["sm_o"], 1)
            pe.wait_ge(s["sm_done"], SB)
            for g in range(8):
                if g >= 4:
                    pe.wait_ge(s["xm_done"], g - 3)
                for h in (2 * (g // 2), 2 * (g // 2) + 1):
                    o = 64 * (h % 2)
                    last = nc.tensor.matmul(ps[o:o + 64, g % 4, 0:HALF], wuv[:, h * VD:(h + 1) * VD], olT[:, h, half(g % 2)],
                                            start=True, stop=True)
                last.then_inc(s["xm_ps"], 1)
            pe.wait_ge(s["ml_gated"], TI)
            for i in range(TI):
                pe.wait_ge(s["xm_done"], 5 + i)
                for h in range(MH):
                    last = nc.tensor.transpose(ps[:, (8 + i) % 4, h * TR:(h + 1) * TR], zo[:, i, h * 128:(h + 1) * 128],
                                               ident[0:TR, 0:TR])
                last.then_inc(s["xm_ps"], 1)
            pe.wait_ge(s["wo_in"], 16)
            pe.wait_ge(s["xm_done"], 13)
            for g in range(2 * TI):
                if g >= 4:
                    pe.wait_ge(s["res_done"], g - 3)
                for k in range(KD):
                    last = nc.tensor.matmul(ps[0:TR, g % 4, :], xm[:, k, tile(g // 2)],
                                            wo[:, k, (g % 2) * 512:(g % 2 + 1) * 512], start=(k == 0), stop=(k == KD - 1))
                last.then_inc(s["wo_ps"], 1)
                if g % 2 and g > 1:
                    hidden_transposes(TI + g // 2 - 1)
            hidden_transposes(2 * TI - 1)
            pe.wait_ge(s["ht_done"], 2 * TI)
            pe.wait_ge(s["res_done"], 2 * TI)
            pe.wait_ge(s["sk_in"], 16)
            for hp in range(2 * PH):
                c = hp // 4
                pe.wait_ge(pq_in[c % 2], 16 * (c // 2 + 1))
                for n in range(2):
                    if 2 * hp + n >= 4:
                        pe.wait_ge(s["pq_done"], 2 * hp + n - 3)
                    for k in range(KD):
                        last = nc.tensor.matmul(ps[:, (2 * hp + n) % 4, 0:HALF], wpq[c % 2][:, k, (hp % 4) * 128:(hp % 4 + 1) * 128],
                                                hT[:, k, half(n)], start=(k == 0), stop=(k == KD - 1))
                    last.then_inc(s["pq_ps"], 1)
                pe.wait_ge(s["pq_done"], 2 * hp + 2)
                if hp >= 2:
                    pe.wait_ge(s["sc_done"], hp - 1)
                for i in range(TI):
                    last = nc.tensor.matmul(ps[0:TR, 4 + 2 * (hp % 2) + i // 4, (i % 4) * 128:(i % 4 + 1) * 128],
                                            pqT[:, hp % 2, tile(i)], skT[:, hp, :], start=True, stop=True)
                last.then_inc(s["sc_ps"], 1)
            pe.wait_ge(s["sc_done"], 16)
            for i in range(TI):
                pe.wait_ge(s["tk_pick"], i + 1)
                if i >= 2:
                    pe.wait_ge(s["pk_done"], i - 1)
                for n in range(3):
                    last = nc.tensor.transpose(ps[:, i % 2, n * TR:(n + 1) * TR], pick[:, n, :], ident[0:TR, 0:TR])
                last.then_inc(s["pk_ps"], 1)

            def gates(p, n_oh, n_free):
                pe.wait_ge(s["oh_ready"], n_oh)
                if n_free is not None:
                    pe.wait_ge(s["g_done"], n_free)
                for t in range(GT):
                    last = nc.tensor.matmul(ps[:, 6 + p, t * NK:(t + 1) * NK], oh[p][:, 0, t, :], oh[p][:, 1, t, :],
                                            start=True, stop=True)
                last.then_inc(s["g_ps"], 1)

            def up(p, n, n_in, n_free):
                pe.wait_ge(u_in[p], n_in)
                if n_free is not None:
                    pe.wait_ge(s["a_done"], n_free)
                for k in range(KD):
                    last = nc.tensor.matmul(ps[:, 6 + p, 0:HALF], ut[p][:, k, :], hT[:, k, half(n)],
                                            start=(k == 0), stop=(k == KD - 1))
                last.then_inc(s["s_ps"], 1)

            def down(p, n_h, n_in, first, last_block):
                pe.wait_ge(s["h_done"], n_h)
                pe.wait_ge(v_in[p], n_in)
                for d, t0, n, bank, col in PIECES:
                    last = nc.tensor.matmul(ps[:, bank, col:col + n], vt[p][:, d * 128:(d + 1) * 128], hb[:, p, t0:t0 + n],
                                            start=(first and col == 0), stop=last_block, skip_group_check=True)
                last.then_inc(s["y_ps"], 1)

            pe.wait_ge(s["pk_done"], TI)
            for n in range(2):
                g0, b0, w0 = n * NG, n * NK, n * NK * 8
                if n == 1:
                    pe.wait_ge(s["a_done"], NK)
                for p in range(2):
                    gates(p, g0 + p + 1, None if n == 0 else g0 + p - 1)
                with pe.Fori(1, NG // 2) as j:
                    for p in range(2):
                        gates(p, j * 2 + (g0 + p + 1), j * 2 + (g0 + p - 1))
                pe.wait_ge(s["g_done"], g0 + NG)
                if n == 1:
                    pe.wait_ge(s["y_done"], 1)
                up(0, n, w0 + 16, b0 - 1 if n else None)
                up(1, n, w0 + 16, b0 if n else None)
                down(0, b0 + 1, w0 + 16, True, False)
                up(0, n, w0 + 32, b0 + 1)
                down(1, b0 + 2, w0 + 16, False, False)
                with pe.Fori(1, NK // 2 - 1) as j:
                    up(1, n, j * 16 + (w0 + 16), j * 2 + b0)
                    down(0, j * 2 + (b0 + 1), j * 16 + (w0 + 16), False, False)
                    up(0, n, j * 16 + (w0 + 32), j * 2 + (b0 + 1))
                    down(1, j * 2 + (b0 + 2), j * 16 + (w0 + 16), False, False)
                up(1, n, w0 + NK * 8, b0 + NK - 2)
                down(0, b0 + NK - 1, w0 + NK * 8, False, False)
                down(1, b0 + NK, w0 + NK * 8, False, True)
            pe.wait_ge(s["y_done"], 2)
            for i in range(TI):
                if i >= 2:
                    pe.wait_ge(s["yt_done"], i - 1)
                for k in range(KD):
                    last = nc.tensor.transpose(ps[0:TR, 2 * (i % 2) + k // 4, (k % 4) * 128:(k % 4 + 1) * 128],
                                               hT[:, k, tile(i)], ident)
                last.then_inc(s["yt_ps"], 1)

        @block.scalar
        def _(act):
            steps = [0]

            def step(ins):
                steps[0] += 1
                ins.then_inc(s["act_step"], 1)
                act.wait_ge(s["act_step"], steps[0])

            def copy(out, in_):
                return nc.scalar.activation(out, in_, ACT.Copy)

            def norm_roots(at):
                for i in range(TI):
                    act.wait_ge(s["var_ready"], at + i + 1)
                    nc.scalar.activation(rstd[:, i:i + 1], rs1, ACT.Sqrt).then_inc(s["std_ready"], 1)
                    if at < 2 * TI and i >= 1:
                        hidden_copies(at + i - 1)
                if at < 2 * TI:
                    hidden_copies(at + TI - 1)

            def hidden_copies(n):
                i = n % TI
                act.wait_ge(s["ht_ps"], n + 1)
                for a in range(2):
                    last = copy(hT[:, 4 * a:4 * a + 4, tile(i)],
                                ps[:, 4 + 2 * (n % 2) + a, 0:4 * TR].rearrange("p (k t) -> p k t", k=4))
                last.then_inc(s["ht_done"], 1)

            act.wait_ge(s["consts_in"], 32)
            norm_roots(0)
            for g in range(28):
                act.wait_ge(s["z_ps"], g + 1)
                c, i = g // TI, g % TI
                if c == 0:
                    ins = copy(z0[:, i, :], ps[0:TR, g % 4, 0:Z0W])
                elif c == 1:
                    ins = nc.scalar.activation(zk[:, i, :], ps[0:TR, g % 4, :], ACT.Copy, scale=float(DH ** -0.5))
                elif c == 2:
                    ins = copy(zv[:, i, :], ps[0:TR, g % 4, :])
                elif c == 3:
                    ins = nc.scalar.activation(zo[:, i, :], ps[0:TR, g % 4, :], ACT.Sigmoid)
                else:
                    ins = copy(mqT[:, (g - 20) // 2, half(g % 2)], ps[:, g % 4, 0:HALF])
                ins.then_inc(s["z_done"], 1)
            act.wait_ge(s["ssq_ready"], 1)
            nc.scalar.activation(ssq, ssq, ACT.Sqrt).then_inc(s["rms_std"], 1)
            for i in range(TI):
                act.wait_ge(s["tt_ps"], i + 1)
                for a in range(2):
                    last = copy(tt[:, 4 * a:4 * a + 4, tile(i)],
                                ps[:, 4 + 2 * (i % 2) + a, 0:4 * TR].rearrange("p (k t) -> p k t", k=4))
                last.then_inc(s["tt_done"], 1)
            for g in range(29):
                act.wait_ge(s["q_ps"], g + 1)
                if g < 8:
                    ins = copy(qnT[:, g // 2, half(g % 2)], ps[:, g % 4, 0:HALF])
                elif g < 13:
                    ins = copy(qrk[:, g - 8, :], ps[0:TR, g % 4, 0:NH * ROPE])
                else:
                    ins = copy(qlT[:, (g - 13) // 2, half((g - 13) % 2)], ps[:, g % 4, 0:HALF])
                ins.then_inc(s["q_done"], 1)
            for i in range(TI):
                act.wait_ge(s["qrt_ps"], i + 1)
                copy(qrT[:, :, tile(i)], ps[:, 4 + i % 2, 0:2 * TR].rearrange("p (k t) -> p k t", k=2)).then_inc(s["qrt_done"], 1)
            act.wait_ge(s["ls_abs"], 1)
            step(nc.scalar.activation(glog, gabs, ACT.Exp, scale=-1.0))
            nc.scalar.activation(glog, glog, ACT.Ln, bias=1.0).then_inc(s["ls_log"], 1)
            for i in range(TI):
                act.wait_ge(s["dg_ps"], i + 1)
                copy(cs_bc[:, :, tile(i)], ps[:, 4 + i % 2, 0:MH * TR].rearrange("p (h t) -> p h t", h=MH))\
                    .then_inc(s["csbc_done"], 1)

            def pt_copy(i, par):
                n = min(i + 1, 4) * TR
                last = copy(sbuf_pt[:, par, 0:n], ps[0:TR, 4, 0:n])
                if i == 4:
                    last = copy(sbuf_pt[:, par, n:n + TR], ps[0:TR, 5, 0:TR])
                return last

            def mla_pt(j):
                act.wait_ge(s["mla_tps"], j + 1)
                if j >= 2:
                    act.wait_ge(s["mla_o"], j - 1)
                pt_copy(j // NH, j % 2).then_inc(s["mla_pt"], 1)

            for j in range(NJ + 1):
                if j < NJ:
                    act.wait_ge(s["mla_max"], j + 1)
                    nk = TR * (j // NH + 1)
                    nc.scalar.activation(sbuf_s[:, j % 2, 0:nk], sbuf_s[:, j % 2, 0:nk], ACT.Exp, bias=nb[:, j % 2],
                                         scale=SM_SCALE, accum_out=rsum[:, j % 2]).then_inc(s["mla_exp"], 1)
                if j >= 1:
                    mla_pt(j - 1)

            def ml_pt(n):
                act.wait_ge(s["ml_tps"], n + 1)
                if n >= 2:
                    act.wait_ge(s["ml_num"], n - 1)
                pt_copy(n // MH, n % 2).then_inc(s["ml_pt"], 1)

            for i in range(TI):
                nk = TR * (i + 1)
                act.wait_ge(s["ml_m"], i + 1)
                for h in range(MH):
                    nc.scalar.activation(wexp[:, h, 0:nk], wexp[:, h, 0:nk], ACT.Exp, bias=nm[:, i, h:h + 1]).then_inc(s["ml_w"], 1)
                nc.scalar.activation(emm[:, i, :], mabs[:, i, :], ACT.Exp, scale=-1.0)
                nc.scalar.activation(am[:, i, :], am[:, i, :], ACT.Exp).then_inc(s["ml_w"], 1)
                for h in range(MH):
                    ml_pt(i * MH + h)
                act.wait_ge(s["hvar"], i + 1)
                nc.scalar.activation(rs4, rs4, ACT.Sqrt).then_inc(s["hstd"], 1)
            act.wait_ge(s["ws_lin"], 1)
            nc.scalar.activation(wsp, wsp, ACT.Exp).then_inc(s["ws_exp"], 1)
            act.wait_ge(s["sws_lin"], 1)
            nc.scalar.activation(wss, wss, ACT.Exp).then_inc(s["sws_exp"], 1)
            for b in range(SB):
                act.wait_ge(s["sm_max"], b + 1)
                if b >= 1:
                    act.wait_ge(s["sm_tps"], b)
                step(nc.scalar.activation(s_p[:, 0:2048].rearrange("p (a b) -> p a b", a=4), ps[0:NS, 0:4, :], ACT.Exp,
                                          bias=smx[:, 2:3], scale=SM_SCALE, accum_out=smx[:, 0:1]))
                nc.scalar.activation(s_p[:, 2048:2080], s_p[:, 2048:2080], ACT.Exp, bias=smx[:, 2:3], scale=SM_SCALE,
                                     accum_out=smx[:, 1:2]).then_inc(s["sm_exp"], 1)
                act.wait_ge(s["sm_tps"], b + 1)
                if b >= 1:
                    act.wait_ge(s["sm_o"], b)
                copy(s_pt[:, 0:PAGES, :], ps[:, 5, :].rearrange("p (k q) -> p k q", k=PAGES))
                copy(s_pt[0:NS, PAGES, :], ps[0:NS, 6, 0:NS]).then_inc(s["sm_pt"], 1)
            for g in range(13):
                act.wait_ge(s["xm_ps"], g + 1)
                if g < 8:
                    ins = copy(xm[:, g // 2, half(g % 2)], ps[:, g % 4, 0:HALF])
                else:
                    ins = copy(xm[:, 4:8, tile(g - 8)], ps[:, g % 4, 0:MH * TR].rearrange("p (h t) -> p h t", h=MH))
                ins.then_inc(s["xm_done"], 1)
            norm_roots(TI)
            for hp in range(2 * PH):
                if hp >= 2:
                    act.wait_ge(s["sc_ps"], hp - 1)
                for n in range(2):
                    act.wait_ge(s["pq_ps"], 2 * hp + n + 1)
                    copy(pqT[:, hp % 2, half(n)], ps[:, (2 * hp + n) % 4, 0:HALF]).then_inc(s["pq_done"], 1)
            for i in range(TI):
                act.wait_ge(s["tk_lin"], i + 1)
                nc.scalar.activation(cv, cv, ACT.Exp).then_inc(s["tk_exp"], 1)
                act.wait_ge(s["pk_ps"], i + 1)
                copy(pickT[:, :, tile(i)], ps[:, i % 2, 0:3 * TR].rearrange("p (k t) -> p k t", k=3)).then_inc(s["pk_done"], 1)

            def gate_copy(p, g, n):
                act.wait_ge(s["g_ps"], n)
                copy(gm[:, bass.ds(g * GT, GT), :], ps[:, 6 + p, :].rearrange("p (t e) -> p t e", t=GT)).then_inc(s["g_done"], 1)

            def gelu(p, n_s, n_free):
                act.wait_ge(s["s_ps"], n_s)
                if n_free is not None:
                    act.wait_ge(s["h_done"], n_free)
                nc.scalar.activation(ab[:, p, :], ps[:, 6 + p, 0:HALF], ACT.Gelu_apprx_tanh).then_inc(s["a_done"], 1)

            for n in range(2):
                if n == 1:
                    act.wait_ge(s["h_done"], NK)
                with act.Fori(0, NG // 2) as j:
                    for p in range(2):
                        gate_copy(p, j * 2 + p, j * 2 + (n * NG + p + 1))
                for p in range(2):
                    gelu(p, n * NK + p + 1, None if n == 0 else NK + p - 1)
                with act.Fori(1, NK // 2) as j:
                    for p in range(2):
                        gelu(p, j * 2 + (n * NK + p + 1), j * 2 + (n * NK + p - 1))
            norm_roots(2 * TI)

        @block.vector
        def _(dve):
            steps = [0]
            v = nc.vector

            def step(ins):
                steps[0] += 1
                ins.then_inc(s["dve_step"], 1)
                dve.wait_ge(s["dve_step"], steps[0])

            def layer_norm(row, i, n, g, b):
                for a in range(2):
                    ins = v.bn_stats(st6[:, a, :], row[:, a * 512:(a + 1) * 512])
                step(ins)
                step(v.bn_aggr(mv2, st6[:, 0:2, :]))
                v.tensor_scalar(rs1, mv2[:, 1:2], 1e-5, None, ALU.add).then_inc(s["var_ready"], 1)
                dve.wait_ge(s["std_ready"], n + 1)
                step(v.reciprocal(rstd[:, i:i + 1], rstd[:, i:i + 1]))
                step(v.tensor_scalar(row, row, mv2[:, 0:1], rstd[:, i:i + 1], ALU.subtract, ALU.mult))
                step(v.tensor_tensor(row, row, g, ALU.mult))
                v.tensor_tensor(row, row, b, ALU.add).then_inc(s["ln_done"], 1)

            dve.wait_ge(s["consts_in"], 32)
            dve.wait_ge(s["x_in"], 16)
            dve.wait_ge(s["ln_in"], 16)
            for i in range(TI):
                layer_norm(hid[:, i, :], i, i, lnv[:, 0, :], lnv[:, 1, :])
            dve.wait_ge(s["z_done"], TI)
            for i in range(TI):
                ckv, cq = z0[:, i, QR:QR + KVR], z0[:, i, 0:QR]
                v.tensor_tensor_reduce(junk[:, 0:KVR], ckv, ckv, 1.0, 0.0, ALU.mult, ALU.add, ssq[:, i, 0:1])
                step(v.tensor_tensor_reduce(junk[:, 256:512], cq, cq, 1.0, 0.0, ALU.mult, ALU.add, ssq[:, i, 1:2]))
            v.tensor_scalar(ssq[:, :, 0], ssq[:, :, 0], 1.0 / KVR, 1e-6, ALU.mult, ALU.add)
            v.tensor_scalar(ssq[:, :, 1], ssq[:, :, 1], 1.0 / QR, 1e-6, ALU.mult, ALU.add).then_inc(s["ssq_ready"], 1)
            x1, x2 = z0[:, :, QR + KVR:QR + KVR + 16], z0[:, :, QR + KVR + 16:QR + KVR + 32]
            t4 = [rtmp[:, n].rearrange("p (i r) -> p i r", i=TI) for n in range(4)]
            v.tensor_tensor(t4[0], x1, cos, ALU.mult)
            v.tensor_tensor(t4[1], x2, sin, ALU.mult)
            v.tensor_tensor(t4[2], x1, sin, ALU.mult)
            step(v.tensor_tensor(t4[3], x2, cos, ALU.mult))
            v.tensor_tensor(x1, t4[0], t4[1], ALU.subtract)
            step(v.tensor_tensor(x2, t4[2], t4[3], ALU.add))
            for c in range(4):
                v.tensor_copy(kp4[:, :, c, :], z0[:, :, QR + KVR:QR + KVR + ROPE])
            dve.wait_ge(s["rms_std"], 1)
            step(v.reciprocal(ssq, ssq))
            for i in range(TI):
                ckv, cq = z0[:, i, QR:QR + KVR], z0[:, i, 0:QR]
                v.scalar_tensor_tensor(ckv, ckv, ssq[:, i, 0:1], const("kvg", rows=TR), ALU.mult, ALU.mult)
                ins = v.scalar_tensor_tensor(cq, cq, ssq[:, i, 1:2], const("qg", rows=TR), ALU.mult, ALU.mult)
            ins.then_inc(s["tok_done"], 1)
            dve.wait_ge(s["q_done"], 13)
            dve.wait_ge(s["ln_done"], TI)
            for i in range(TI):
                qv = qrk[:, i, :].rearrange("p (h r) -> p h r", h=NH)
                a, b = qv[:, :, 0:16], qv[:, :, 16:32]
                ci, si = bc(cos[:, i, :], 1, NH), bc(sin[:, i, :], 1, NH)
                v.tensor_tensor(rqt[:, 0], a, ci, ALU.mult)
                v.tensor_tensor(rqt[:, 1], b, si, ALU.mult)
                v.tensor_tensor(rqt[:, 2], a, si, ALU.mult)
                step(v.tensor_tensor(rqt[:, 3], b, ci, ALU.mult))
                v.tensor_tensor(a, rqt[:, 0], rqt[:, 1], ALU.subtract)
                ins = v.tensor_tensor(b, rqt[:, 2], rqt[:, 3], ALU.add)
                ins.then_inc(s["rot_done"], 1)
                dve.wait_ge(s["rot_done"], i + 1)
            q0 = qrk[0:NS, 0, :].rearrange("p (h r) -> p h r", h=NH)
            for c in range(4):
                ins = v.tensor_copy(qrc[:, :, c, :], q0)
            ins.then_inc(s["qrc_ready"], 1)
            dve.wait_ge(s["q_done"], 29)
            v.tensor_copy(qs.rearrange("p b (h t) -> p b h t", h=NH),
                          qlT[:, :, 0:NS].rearrange("p h (b t) -> p b h t", b=SB))
            dve.wait_ge(s["qrs_ps"], 1)
            v.tensor_copy(qrs4.rearrange("p b (h t) -> p b h t", h=NH),
                          ps[:, 6, 0:256].rearrange("p (h b t) -> p b h t", h=NH, b=SB)).then_inc(s["qs_ready"], 1)
            step(v.tensor_tensor(gat, z0[:, :, QR + KVR + ROPE:Z0W], bc(const("bg", rows=TR), 1, TI), ALU.add))
            v.scalar_tensor_tensor(gabs, gat[:, :, MH:2 * MH], -1.0, gat[:, :, MH:2 * MH], ALU.mult, ALU.max).then_inc(s["ls_abs"], 1)
            step(v.tensor_scalar(lf, gat[:, :, MH:2 * MH], 0.0, None, ALU.min))
            dve.wait_ge(s["ls_log"], 1)
            v.tensor_tensor(lf, lf, glog, ALU.subtract).then_inc(s["lf_ready"], 1)
            dve.wait_ge(s["cum_ps"], 1)
            step(v.tensor_copy(cum, ps[0:TR, 7, 0:TI * MH].rearrange("p (i h) -> p i h", i=TI)))
            step(v.tensor_tensor(cs, gat[:, :, 0:MH], cum, ALU.subtract))
            dve.wait_ge(s["z_ps"], 28)
            for i in range(TI):
                if i >= 2:
                    dve.wait_ge(s["dg_ps"], i - 1)
                v.tensor_tensor(dg[:, i % 2], bc(ident[0:TR, 0:TR], 1, MH), bc(cs[:, i, :], 2, TR), ALU.mult)\
                    .then_inc(s["dg_ready"], 1)

            def mla_max(j):
                nk = TR * (j // NH + 1)
                dve.wait_ge(s["mla_s"], j + 1)
                if j >= 2:
                    dve.wait_ge(s["mla_tps"], j - 1)
                src = ps[0:TR, 2 * (j % 2):2 * (j % 2) + 2, :].rearrange("p a b -> p (a b)")[:, 0:nk]
                step(v.tensor_tensor_reduce(sbuf_s[:, j % 2, 0:nk], src, mask[:, j // NH, 0:nk], 1.0, -3e38,
                                            ALU.add, ALU.max, mx1[:, j % 2]))
                v.tensor_scalar(nb[:, j % 2], mx1[:, j % 2], -SM_SCALE, None, ALU.mult).then_inc(s["mla_max"], 1)

            def mla_norm(j):
                nk = TR * (j // NH + 1)
                dve.wait_ge(s["mla_exp"], j + 1)
                step(v.reciprocal(rrec[:, j % 2], rsum[:, j % 2]))
                v.tensor_scalar(sbuf_s[:, j % 2, 0:nk], sbuf_s[:, j % 2, 0:nk], rrec[:, j % 2], None, ALU.mult)\
                    .then_inc(s["mla_p"], 1)

            def mla_copy(j):
                dve.wait_ge(s["mla_o"], j + 1)
                v.tensor_copy(olT[:, j % NH, tile(j // NH)], ps[:, 6 + j % 2, 0:TR]).then_inc(s["mla_done"], 1)

            dve.wait_ge(s["dg_ps"], TI)
            dve.wait_ge(s["z_done"], 28)
            for j in range(NJ + 3):
                if j < NJ:
                    mla_max(j)
                if 1 <= j <= NJ:
                    mla_norm(j - 1)
                if j >= 3:
                    mla_copy(j - 3)
            dve.wait_ge(s["inter_ps"], 1)
            v.tensor_copy(numT, ps[:, 6, 0:128].rearrange("p (h t) -> p h t", h=MH)).then_inc(s["numt_done"], 1)
            step(v.tensor_tensor(nq, ps[0:NS, 6, 256:288].rearrange("p (h b) -> p h b", h=MH),
                                 bc(const("selb", rows=NS), 1, MH), ALU.mult))
            step(v.tensor_reduce(nqs, nq, AX, ALU.add))
            dve.wait_ge(s["numi_ps"], 1)
            v.tensor_copy(numi, ps[0:NS, 7, :].rearrange("p (h v) -> p h v", h=MH)).then_inc(s["inter_done"], 1)
            dve.wait_ge(s["csbc_done"], TI)
            m0 = const("m0", TI, MH, rows=TR)
            for i in range(TI):
                nk = TR * (i + 1)
                if i >= 1:
                    dve.wait_ge(s["ml_tps"], MH * i)
                for h in range(MH):
                    ins = v.tensor_tensor_reduce(wexp[:, h, 0:nk], cs_bc[0:TR, h, 0:nk], mask[:, i, 0:nk], 1.0, -3e38,
                                                 ALU.add, ALU.max, mx4[:, h:h + 1])
                step(ins)
                step(v.tensor_tensor(mm[:, i, :], mx4, m0[:, i, :], ALU.max))
                v.tensor_scalar(nm[:, i, :], mm[:, i, :], -1.0, None, ALU.mult)
                v.tensor_tensor(mabs[:, i, :], cum[:, i, :], mm[:, i, :], ALU.add)
                v.tensor_tensor(am[:, i, :], m0[:, i, :], mm[:, i, :], ALU.subtract).then_inc(s["ml_m"], 1)
                for h in range(MH):
                    n = i * MH + h
                    dve.wait_ge(s["ml_w"], (MH + 1) * i + h + 1)
                    dve.wait_ge(s["ml_qk"], n + 1)
                    src = ps[0:TR, 2 * (n % 2):2 * (n % 2) + 2, :].rearrange("p a b -> p (a b)")[:, 0:nk]
                    v.tensor_tensor_reduce(wexp[:, h, 0:nk], src, wexp[:, h, 0:nk], 1.0, 0.0, ALU.mult, ALU.add,
                                           den[:, h:h + 1]).then_inc(s["ml_p"], 1)
                dve.wait_ge(s["ml_p"], MH * (i + 1))
                dve.wait_ge(s["ml_w"], (MH + 1) * (i + 1))
                if i == 0:
                    step(v.tensor_tensor(nqs, nqs, am[0:NS, 0, :], ALU.mult))
                    v.tensor_tensor(numi, numi, bc(am[0:NS, 0, :], 2, DH), ALU.mult)
                    step(v.tensor_tensor(den[0:NS], den[0:NS], nqs, ALU.add))
                step(v.scalar_tensor_tensor(den, den, -1.0, den, ALU.mult, ALU.max))
                step(v.tensor_tensor(den, den, emm[:, i, :], ALU.max))
                step(v.reciprocal(rden, den))
                dve.wait_ge(s["ml_num"], MH * (i + 1))
                num = ps[0:TR, 6, :].rearrange("p (h v) -> p h v", h=MH)
                if i == 0:
                    step(v.tensor_copy(hbuf, num))
                    step(v.tensor_tensor(hbuf[0:NS], hbuf[0:NS], numi, ALU.add))
                    num = hbuf
                v.tensor_tensor(hbuf, num, bc(rden, 2, DH), ALU.mult).then_inc(s["ml_h"], 1)
                dve.wait_ge(s["ml_h"], i + 1)
                for h in range(MH):
                    ins = v.bn_stats(st6[:, h, :], hbuf[:, h, :])
                step(ins)
                for h in range(MH):
                    ins = v.bn_aggr(mvh[:, h, :], st6[:, h:h + 1, :])
                step(ins)
                v.tensor_scalar(rs4, mvh[:, :, 1], 1e-5, None, ALU.add).then_inc(s["hvar"], 1)
                dve.wait_ge(s["hstd"], i + 1)
                step(v.reciprocal(rs4, rs4))
                for h in range(MH):
                    ins = v.tensor_scalar(hbuf[:, h, :], hbuf[:, h, :], mvh[:, h, 0:1], rs4[:, h:h + 1],
                                          ALU.subtract, ALU.mult)
                step(ins)
                hf = hbuf.rearrange("p h v -> p (h v)")
                step(v.tensor_tensor(hf, hf, const("mhg", rows=TR), ALU.mult))
                v.tensor_tensor(zo[:, i, :], zo[:, i, :], hf, ALU.mult).then_inc(s["ml_gated"], 1)
            dve.wait_ge(s["mlast_ps"], 1)
            v.tensor_copy(mlast, ps[0:NS, 7, 8:8 + MH])
            step(v.tensor_copy(nml, ps[:, 7, 0:MH]))
            v.tensor_tensor(wsp, cs, bc(nml[0:TR, :], 1, TI), ALU.subtract).then_inc(s["ws_lin"], 1)
            v.tensor_tensor(wss, cs[0:NS, 0, :], mlast, ALU.subtract).then_inc(s["sws_lin"], 1)
            dve.wait_ge(s["ml_pt"], TI * MH)
            v.tensor_tensor(sR, bc(am[0:NS, 0, :], 2, SB), bc(const("lastb", rows=NS), 1, MH), ALU.mult).then_inc(s["sel_ready"], 1)
            dve.wait_ge(s["ws_exp"], 1)
            v.tensor_scalar(wsp[:, 0, :], wsp[:, 0, :], const("pmask", rows=TR), None, ALU.mult).then_inc(s["wsp_done"], 1)
            dve.wait_ge(s["wsp_done"], 1)
            for i in range(TI):
                if i >= 2:
                    dve.wait_ge(s["cst_ps"], i - 1)
                v.tensor_tensor(vw[:, i % 2].rearrange("p (h v) -> p h v", h=MH),
                                zv[:, i, :].rearrange("p (h v) -> p h v", h=MH), bc(wsp[:, i, :], 2, DH), ALU.mult)\
                    .then_inc(s["vw_ready"], 1)
            dve.wait_ge(s["cst_ps"], TI)
            dve.wait_ge(s["ml_num"], TI * MH)
            v.tensor_copy(cst[:, 0:512], ps[:, 0, :])
            v.tensor_copy(cst[:, 512:516], ps[:, 1, 0:MH]).then_inc(s["cst_done"], 1)
            dve.wait_ge(s["sws_exp"], 1)
            v.tensor_tensor(wsb, bc(wss, 2, SB), bc(const("selb", rows=NS), 1, MH), ALU.mult).then_inc(s["wsb_done"], 1)
            dve.wait_ge(s["wsb_done"], 1)
            dve.wait_ge(s["sel_ps"], 1)
            step(v.tensor_copy(aLb, ps[:, 7, 16:48]))
            nf = nst.rearrange("p h b -> p (h b)")
            dve.wait_ge(s["sst_ps"], 1)
            step(v.tensor_tensor(nf, nf, aLb, ALU.mult))
            v.tensor_tensor(nf, nf, ps[:, 6, 0:32], ALU.add).then_inc(s["sst_done"], 1)

            def state_values(b):
                if b >= 2:
                    dve.wait_ge(s["sst_ps"], b)
                v.tensor_tensor(vw[0:NS, b % 2].rearrange("p (h v) -> p h v", h=MH),
                                zv[0:NS, 0, :].rearrange("p (h v) -> p h v", h=MH), bc(wsb[:, :, b], 2, DH), ALU.mult)\
                    .then_inc(s["vwb_ready"], 1)

            state_values(0)
            for b in range(SB):
                if b + 1 < SB:
                    state_values(b + 1)
                dve.wait_ge(s["sst_ps"], b + 2)
                for h in range(MH):
                    c = h * SB + b
                    ins = v.scalar_tensor_tensor(ct[:, c, :], ct[:, c, :], aLb[:, c:c + 1],
                                                 ps[:, 2 + b % 2, h * 128:(h + 1) * 128], ALU.mult, ALU.add)
                ins.then_inc(s["sst_done"], 1)
            dve.wait_ge(s["ml_tps"], TI * MH)
            for b in range(SB):
                dve.wait_ge(s["sm_s"], b + 1)
                if b >= 1:
                    dve.wait_ge(s["sm_tps"], b)
                v.tensor_reduce(smx[:, 0:1], ps[0:NS, 0:4, :].rearrange("p a b -> p (a b)"), AX, ALU.max)
                step(v.tensor_tensor_reduce(s_p[:, 2048:2080], ps[0:NS, 4, 0:NS], smask[:, b, :], 1.0, -3e38,
                                            ALU.add, ALU.max, smx[:, 1:2]))
                step(v.tensor_tensor(smx[:, 2:3], smx[:, 0:1], smx[:, 1:2], ALU.max))
                v.tensor_scalar(smx[:, 2:3], smx[:, 2:3], -SM_SCALE, None, ALU.mult).then_inc(s["sm_max"], 1)
                dve.wait_ge(s["sm_exp"], b + 1)
                step(v.tensor_tensor(smx[:, 0:1], smx[:, 0:1], smx[:, 1:2], ALU.add))
                step(v.reciprocal(smx[:, 1:2], smx[:, 0:1]))
                v.tensor_scalar(s_p, s_p, smx[:, 1:2], None, ALU.mult).then_inc(s["sm_p"], 1)
                dve.wait_ge(s["sm_p"], b + 1)
                dve.wait_ge(s["sm_o"], b + 1)
                v.tensor_copy(olT[:, :, 4 * b:4 * b + 4], ps[:, 7, 0:NS].rearrange("p (h t) -> p h t", h=NH)).then_inc(s["sm_done"], 1)
            dve.wait_ge(s["ln1_in"], 16)
            for i in range(TI):
                for n in range(2):
                    dve.wait_ge(s["wo_ps"], 2 * i + n + 1)
                    seg = hid[:, i, n * 512:(n + 1) * 512]
                    v.scalar_tensor_tensor(seg, seg, ALPHA, ps[0:TR, (2 * i + n) % 4, :], ALU.mult, ALU.add)\
                        .then_inc(s["res_done"], 1)
                dve.wait_ge(s["res_done"], 2 * i + 2)
                layer_norm(hid[:, i, :], i, TI + i, lnv[:, 0, :], lnv[:, 1, :])
            dve.wait_ge(s["ht_ps"], 2 * TI)
            for hp in range(2 * PH):
                dve.wait_ge(s["sc_ps"], hp + 1)
                b = 4 + 2 * (hp % 2)
                v.tensor_copy(sc[:, 0:4, hp, :], ps[0:TR, b, :].rearrange("p (i k) -> p i k", i=4))
                v.tensor_copy(sc[:, 4, hp, :], ps[0:TR, b + 1, 0:128]).then_inc(s["sc_done"], 1)

            def top16(vals, idx, src, scratch):
                step(v.max(vals[:, 0:8], src))
                v.max_index(idx[:, 0:8], vals[:, 0:8], src)
                step(v.match_replace(scratch, vals[:, 0:8], src, -BIG))
                step(v.max(vals[:, 8:16], scratch))
                step(v.max_index(idx[:, 8:16], vals[:, 8:16], scratch))

            dve.wait_ge(s["sc_done"], 16)
            dve.wait_ge(s["wo_ps"], 2 * TI)
            for i in range(TI):
                for q in range(2 * PH):
                    top16(sv[:, q, :], siu[:, q, :], sc[:, i, q, :], tks[:, 0:NK])
                v.tensor_copy(sif, siu)
                for h in range(PH):
                    step(v.tensor_tensor(cand.rearrange("p (a b) -> p a b", a=TOPK), bc(sv[:, 2 * h, :], 2, TOPK),
                                         bc(sv[:, 2 * h + 1, :], 1, TOPK), ALU.add))
                    top16(cv[:, h, :], ciu[:, h, :], cand, tks)
                step(v.tensor_copy(tsum, cv[:, :, 0]))
                v.tensor_tensor(cv, cv, bc(tsum, 2, TOPK), ALU.subtract).then_inc(s["tk_lin"], 1)
                cf = ciu.rearrange("p h k -> p (h k)")
                v.tensor_scalar(cau[:, 0], cf, 4, None, ALU.logical_shift_right)
                step(v.tensor_scalar(cau[:, 1], cf, 15, None, ALU.bitwise_and))
                step(v.tensor_copy(ca, cau))
                if i >= 1:
                    dve.wait_ge(s["pk_ps"], i)
                for p in range(2):
                    keys = sif.rearrange("p (h t) j -> p h t j", t=2)[:, :, p, :]
                    step(v.tensor_tensor(eq, bc(ca[:, p].rearrange("p (h k) -> p h k", h=PH), 3, TOPK),
                                         bc(bc(iota[0:TR, 0:TOPK], 1, TOPK), 1, PH), ALU.is_equal))
                    step(v.tensor_tensor(eq, eq, bc(keys, 2, TOPK), ALU.mult))
                    step(v.tensor_reduce(pick[:, p].rearrange("p (h k) -> p h k", h=PH), eq, AX, ALU.add))
                dve.wait_ge(s["tk_exp"], i + 1)
                step(v.tensor_reduce(tsum, cv, AX, ALU.add))
                step(v.reciprocal(tsum, tsum))
                v.tensor_tensor(pick[:, 2].rearrange("p (h k) -> p h k", h=PH), cv, bc(tsum, 2, TOPK), ALU.mult)\
                    .then_inc(s["tk_pick"], 1)

            def one_hots(p, tok, n_free):
                if n_free is not None:
                    dve.wait_ge(s["g_ps"], n_free)
                v.tensor_copy(pk4[p], pickT[:, :, bass.ds(tok, GT)]).then_inc(s["pk4_done"], 1)

            def one_hot_rows(p, n):
                dve.wait_ge(s["pk4_done"], n)
                for t in range(GT):
                    v.tensor_scalar(oh[p][:, 0, t, :], iota, pk4[p][:, 0, t:t + 1], None, ALU.is_equal)
                    ins = v.tensor_scalar(oh[p][:, 1, t, :], iota, pk4[p][:, 1, t:t + 1], pk4[p][:, 2, t:t + 1],
                                          ALU.is_equal, ALU.mult)
                ins.then_inc(s["oh_ready"], 1)

            def gate(p, blk, n_a, n_free):
                dve.wait_ge(s["a_done"], n_a)
                if n_free is not None:
                    dve.wait_ge(s["y_ps"], n_free)
                v.tensor_tensor(hb[:, p, :], ab[:, p, :], gm[:, :, bass.ds(blk, 1)].rearrange("p t a -> p (t a)"),
                                ALU.mult).then_inc(s["h_done"], 1)

            dve.wait_ge(s["pk_done"], TI)
            for n in range(2):
                g0, b0 = n * NG, n * NK
                for p in range(2):
                    one_hots(p, n * HALF + p * GT, g0 + p - 1 if n else None)
                    one_hot_rows(p, g0 + p + 1)
                with dve.Fori(1, NG // 2) as j:
                    for p in range(2):
                        one_hots(p, j * (2 * GT) + (n * HALF + p * GT), j * 2 + (g0 + p - 1))
                        one_hot_rows(p, j * 2 + (g0 + p + 1))
                dve.wait_ge(s["g_done"], g0 + NG)
                for p in range(2):
                    gate(p, p, b0 + p + 1, b0 + p - 1 if n else None)
                with dve.Fori(1, NK // 2) as j:
                    for p in range(2):
                        gate(p, j * 2 + p, j * 2 + (b0 + p + 1), j * 2 + (b0 + p - 1))
                dve.wait_ge(s["y_ps"], b0 + NK)
                for d, t0, m, bank, col in PIECES:
                    seg = hT[:, d, n * HALF + t0:n * HALF + t0 + m]
                    ins = v.scalar_tensor_tensor(seg, seg, ALPHA, ps[:, bank, col:col + m], ALU.mult, ALU.add)
                ins.then_inc(s["y_done"], 1)
            dve.wait_ge(s["ln2_in"], 16)
            for i in range(TI):
                dve.wait_ge(s["yt_ps"], i + 1)
                b = 2 * (i % 2)
                v.tensor_copy(yt[:, i, :].rearrange("p (a b) -> p a b", a=2), ps[0:TR, b:b + 2, :]).then_inc(s["yt_done"], 1)
                dve.wait_ge(s["yt_done"], i + 1)
                layer_norm(yt[:, i, :], i, 2 * TI + i, lnv2[:, 0, :], lnv2[:, 1, :])


def shape_constants():
    import numpy as np

    c = {k: np.zeros((128, n), np.float32) for k, n in CONSTS.items()}
    c["ident"][:] = np.eye(128)
    c["iota"][:] = np.arange(128)
    c["ones"][:] = 1
    t = np.arange(NT)
    seq = np.where(t < NS, t // SS, -1)
    may = (seq[:, None] == seq[None, :]) & (t[None, :] <= t[:, None])
    m = np.where(may, 0, -BIG).astype(np.float32).reshape(TI, TR, NT).transpose(1, 0, 2)
    c["mask"][:TR] = m.reshape(TR, -1)
    c["ltd0"][:TR] = may[:TR, :TR].T
    c["ltdc"][:TR] = np.triu(np.ones((TR, TR)))
    c["lt01"][NS:TR] = 1
    r = np.arange(NH * SS) % SS
    k = np.arange(NS)
    c["smask"][:NS] = np.stack([np.where((k[None] // SS == b) & (k[None] % SS <= r[:, None]), 0, -BIG)
                                for b in range(SB)], 1).reshape(NS, -1)
    c["sellast"][TR - 1] = 1
    c["lsel"][:NS] = (k[:, None] == (k[None] // SS) * SS + SS - 1)
    c["selb"][:NS] = k[:, None] // SS == np.arange(SB)[None]
    c["lastb"][:NS] = k[:, None] == np.arange(SB)[None] * SS + SS - 1
    c["pmask"][NS:] = 1
    past = PAGES * PAGE
    pos = np.concatenate([past + k % SS, np.arange(NPR)]).astype(np.float32)
    inv = np.float32(10000.0) ** (-np.arange(16, dtype=np.float32) / np.float32(16))
    ang = (pos[:, None] * inv.astype(np.float32)).astype(np.float32)
    for name, f in (("cos", np.cos), ("sin", np.sin)):
        c[name][:TR] = f(ang).astype(np.float32).reshape(TI, TR, 16).transpose(1, 0, 2).reshape(TR, -1)
    return np.concatenate([c[k] for k in CONSTS], axis=1)


def kernel(**inputs):
    import concourse.bacc as bacc
    import numpy as np
    from concourse.bass_utils import run_bass_kernel_spmd

    a = {k: np.asarray(v) for k, v in inputs.items()}

    def rows(*vs):
        return np.ascontiguousarray(np.stack([np.broadcast_to(v.reshape(-1), (128, v.size)) for v in vs], 1))

    def tiles(w):
        return w.reshape(-1, 128, w.shape[1]).transpose(1, 0, 2)

    x = np.concatenate([a["x_sample"].reshape(NS, D), a["meta_tokens"], a["x_prompt"].reshape(-1, D)])
    m0 = np.zeros((NT, MH), np.float32)
    m0[:NS] = np.repeat(a["state_m"][0], SS, axis=0)
    m0 = m0.reshape(TI, TR, MH).transpose(1, 0, 2).reshape(TR, -1)
    m0 = np.concatenate([m0, np.zeros((128 - TR, m0.shape[1]), np.float32)])
    vecs = np.concatenate([rows(a[n])[:, 0] for n in ("q_norm_g", "kv_norm_g", "mh_norm_g", "b_gates")] + [m0], axis=1)
    w = a["w_in"][0]
    o_kr, o_mq = QR + KVR, QR + KVR + ROPE
    mw = MH * DH
    z0w = np.concatenate([w[:, :o_mq], w[:, o_mq + 4 * mw:], np.zeros((D, 512 - Z0W), np.float32)], axis=1)
    order = [z0w] + [w[:, o_mq + n * mw:o_mq + (n + 1) * mw] for n in (1, 2, 3, 0)]
    w_in = np.stack([tiles(c) for c in order])
    qb = a["w_qb"][0].reshape(QR, NH, NOPE + ROPE)
    w_qb = tiles(np.concatenate([qb[:, :, :NOPE].reshape(QR, -1), qb[:, :, NOPE:].reshape(QR, -1)], axis=1))
    kvb = a["w_kvb"][0].reshape(KVR, NH, NOPE + VD)
    w_uk = kvb[:, :, :NOPE].transpose(1, 2, 0).reshape(4, 128, KVR).transpose(1, 0, 2)
    w_uv = kvb[:, :, NOPE:].reshape(KVR, -1)
    w_pq = a["w_pq"][0].reshape(KD, 128, 4, 512).transpose(2, 1, 0, 3)
    sub_keys = a["sub_keys"][0].reshape(16, NK, 128).transpose(2, 0, 1)
    eu = a["expert_u"][0].reshape(NK, NK, KD, 128).transpose(1, 3, 2, 0)
    ev = a["expert_v"][0].reshape(NK, NK, D).transpose(1, 0, 2)
    ins = dict(
        x=x, consts=shape_constants(), vecs=vecs, lnin=rows(a["ln_in_g"], a["ln_in_b"]),
        ln1=rows(a["ln1_g"], a["ln1_b"]), ln2=rows(a["ln2_g"], a["ln2_b"]), w_in=w_in, w_qb=w_qb, w_uk=w_uk, w_uv=w_uv,
        w_o=tiles(a["w_o"][0]), w_pq=w_pq, sub_keys=sub_keys, eu=eu, ev=ev,
        cache_t=a["cache_ckv"][0].transpose(0, 2, 1), cache_n=a["cache_ckv"][0], cache_r=a["cache_kpe"][0].transpose(0, 2, 1),
        pages=a["page_table"].reshape(1, -1).astype(np.int32),
        ct0=a["state_C"][0].transpose(3, 1, 0, 2).reshape(DH, MH * SB, DH), nt0=a["state_n"][0].transpose(2, 1, 0))
    outs = dict(o_y=(NT, D), o_ckv=(NT, KVR), o_kpe=(NT, ROPE), o_c=(DH, MH * DH), o_n=(DH, MH), o_m=(NT, MH),
                o_cs=(DH, MH * SB, DH), o_ns=(DH, MH, SB))
    nc = bacc.Bacc("TRN2", target_bir_lowering=False, num_devices=1)
    arrays, args = {}, []
    for name, v in ins.items():
        v = np.ascontiguousarray(v)
        arrays[name] = v
        args.append(nc.dram_tensor(name, v.shape, mybir.dt.from_np(v.dtype), kind="ExternalInput").ap())
    for name, shape in outs.items():
        args.append(nc.dram_tensor(name, shape, F32, kind="ExternalOutput").ap())
    build(nc, *args)
    r = run_bass_kernel_spmd(nc, [arrays], core_ids=[0]).results[0]
    y, ckv, kpe, m = r["o_y"], r["o_ckv"], r["o_kpe"], r["o_m"]
    c_p = r["o_c"].reshape(DH, MH, DH).transpose(1, 2, 0)
    c_s = r["o_cs"].reshape(DH, MH, SB, DH).transpose(2, 1, 3, 0)
    return (y[NS + 16:][None], y[:NS].reshape(SB, SS, D),
            ckv[NS:][None, None], kpe[NS:][None, None], np.ascontiguousarray(c_p)[None, None],
            np.ascontiguousarray(r["o_n"].T)[None, None], m[-1][None, None],
            ckv[:NS].reshape(1, SB, SS, KVR), kpe[:NS].reshape(1, SB, SS, ROPE), np.ascontiguousarray(c_s)[None],
            np.ascontiguousarray(r["o_ns"].transpose(2, 1, 0))[None], m[SS - 1:NS:SS][None])
```

```python
from contextlib import ExitStack

import concourse.bass as bass
from concourse import mybir

ALU = mybir.AluOpType
ACT = mybir.ActivationFunctionType
F32 = mybir.dt.float32
F32R = mybir.dt.float32r
I32 = mybir.dt.int32
U32 = mybir.dt.uint32
AX = mybir.AxisListType.X

D = 1024
KD = D // 128
NS = 32
SB, SS = 8, 4
NPR = 528
NT = NS + NPR
TR = 112
TI = NT // TR
HALF = NT // 2
NH, NOPE, ROPE, VD = 8, 64, 32, 64
MH, DH = 4, 128
QR, KVR = 256, 128
SM_SCALE = float((NOPE + ROPE) ** -0.5)
PAGES, PAGE = 16, 128
PH, NK, TOPK = 8, 128, 16
ALPHA = float(2.0 ** 0.25)
BIG = 1e30
EC = 32
ROUNDS = NK // EC
PT = (256, NT - 256)
T0 = (0, PT[0])
PM = max(PT)
PAIR = tuple(n // (EC // 2) for n in PT)
GTS = tuple((n - n // 2, n // 2) for n in PAIR)
GTM = max(map(max, GTS))
RECORD = KVR + PAGE + PAGE // 4
Z0W = QR + KVR + ROPE + 2 * MH

CONSTS = dict(ident=128, iota=128, ones=128, mask=TI * NT, ltd0=TR, ltdc=TR, lt01=TR, smask=SB * NS, sellast=128,
              lsel=NS, selb=SB, lastb=SB, pmask=1, cos=TI * 16, sin=TI * 16)
VECS = dict(qg=QR, kvg=KVR, mhg=MH * DH, bg=2 * MH, m0=TI * MH)


def offsets(table, at=0):
    out = {}
    for name, n in table.items():
        out[name] = (at, n)
        at += n
    return out, at


CO, C_END = offsets(CONSTS)
VO, V_END = offsets(VECS, C_END)
SMALL = V_END
XT0 = 5504
BODY = XT0 + KD * NT


def build(nc, x, consts, vecs, lnin, ln1, ln2, w_in, w_qb, w_uk, w_uv, w_o, w_pq, sub_keys,
          eu, ev, cache, pages, ct0, nt0,
          o_y, o_ckv, o_kpe, o_c, o_n, o_m, o_cs, o_ns):
    with ExitStack() as ctx:
        lo = ctx.enter_context(nc.sbuf_tensor("lo", [128, BODY], F32))
        ps = ctx.enter_context(nc.psum_tensor("ps", [128, 8, 512], F32))
        ptab = ctx.enter_context(nc.sbuf_tensor("ptab", [1, SB * PAGES], I32))

        def sem(name):
            return ctx.enter_context(nc.semaphore(name))

        ghr = ctx.enter_context(nc.sbuf_tensor("ghr", [TR, NK], F32R))
        mixer = ExitStack()
        hi = mixer.enter_context(nc.sbuf_tensor("hi", [128, 52900 - BODY], F32))
        mixer.close()

        def view(off, *dims, rows=128, r0=0):
            n = 1
            for d in dims:
                n *= d
            a = lo[r0:r0 + rows, off:off + n] if off < BODY else hi[r0:r0 + rows, off - BODY:off - BODY + n]
            if len(dims) == 1:
                return a
            if len(dims) == 2:
                return a.rearrange("p (a b) -> p a b", a=dims[0])
            if len(dims) == 3:
                return a.rearrange("p (a b c) -> p a b c", a=dims[0], b=dims[1])
            return a.rearrange("p (a b c d) -> p a b c d", a=dims[0], b=dims[1], c=dims[2])

        def const(name, *dims, rows=128):
            off, n = (CO | VO)[name]
            return view(off, *(dims or (n,)), rows=rows)

        ident, iota, ones = const("ident"), const("iota"), const("ones")
        mask = const("mask", TI, NT, rows=TR)
        smask = const("smask", SB, NS, rows=NS)
        cos, sin = const("cos", TI, 16, rows=TR), const("sin", TI, 16, rows=TR)

        small_at = [SMALL]

        def small(*dims, rows=TR):
            n = 1
            for d in dims:
                n *= d
            v = view(small_at[0], *dims, rows=rows)
            small_at[0] += n
            assert small_at[0] <= XT0
            return v

        st6 = small(MH, 6)
        mv2 = small(2)
        mvh = small(MH, 2)
        rstd = small(TI)
        rs1, rs4 = small(1), small(MH)
        gat = small(TI, 2 * MH)
        gabs, glog = small(TI, MH), small(TI, MH)
        lf, cum, cs = small(TI, MH), small(TI, MH), small(TI, MH)
        mm, mabs, nm = small(TI, MH), small(TI, MH), small(TI, MH)
        emm, am = small(TI, MH), small(TI, MH)
        den, rden = small(MH), small(MH)
        mx1, nb, rsum, rrec = small(3, 1), small(3, 1), small(3, 1), small(3, 1)
        nml = small(MH, rows=128)
        wsp = small(TI, MH)
        nq = small(MH, SB, rows=NS)
        ssq = small(TI, 2)
        mx4 = small(MH)
        wss = small(MH, rows=NS)
        smx = small(4, rows=NS)
        nqs = small(MH, rows=NS)
        mlast = small(MH, rows=NS)

        hT = view(XT0, KD, NT)
        cs_bc = view(XT0, MH, NT)
        wexp = view(XT0 + MH * NT, MH, NT, rows=TR)
        H0 = BODY
        hid = view(H0, TI, D, rows=TR)
        LNV = H0 + TI * D
        lnv = view(LNV, 2, D, rows=TR)
        TT0 = LNV + 2 * D
        tt = view(TT0, 8, NT)
        MQ0 = TT0 + 8 * NT
        mqT = view(MQ0, MH, NT)
        Z0 = MQ0 + MH * NT
        z0 = view(Z0, TI, Z0W, rows=TR)
        ZK = Z0 + TI * Z0W
        zkvo = view(ZK, 3, TI, 512, rows=TR)
        zk, zv, zo = zkvo[:, 0], zkvo[:, 1], zkvo[:, 2]
        W0 = ZK + 3 * TI * 512
        wring = view(W0, 2, KD, 512)
        olT = view(W0, NH, NT)
        WQB = W0 + NH * NT
        wqb = view(WQB, 2, NH * (NOPE + ROPE))
        Q0 = W0 + 2 * KD * 512
        qnT = view(Q0, 4, NT)
        sbuf_s = [view(at, NT, rows=TR) for at in (Q0, Q0 + NT, WQB)]
        sbuf_pt = view(Q0 + 2 * NT, 2, NT, rows=TR)
        QRT = Q0 + 4 * NT
        qrT = view(QRT, 2, NT)
        QRK = QRT + 2 * NT
        qrk = view(QRK, TI, NH * ROPE, rows=TR)
        QL = QRK + TI * NH * ROPE
        qlT = view(QL, NH, NT)
        kp4 = view(QL, TI, 4, ROPE, rows=TR)
        junk = view(QL + 640, D, rows=TR)
        rtmp = view(QL + 1664, 4, TI * 16, rows=TR)
        WUK = 51876
        wuk, wuv = view(WUK, 4, 128), view(WUK + 512, NH * VD)
        ct = view(QL, MH * SB, DH)
        cach = [view(at, PAGES, RECORD) for at in (ZK, Q0, Q0 + PAGES * RECORD)]
        qs = view(LNV, SB, NH * SS)
        qrs4 = view(LNV + 256, SB, NH * SS)
        qrc = view(LNV + 512, NH, 4, ROPE, rows=NS)
        nst = view(LNV + 1536, MH, SB)
        numT = view(LNV + 1568, MH, NS)
        numi = view(QRK, MH, DH, rows=NS)
        hbuf = view(QRK + 512, MH, DH, rows=TR)
        rqt = view(LNV, 4, NH, 16, rows=TR)
        dg = view(XT0 + MH * NT, 2, MH, TR, rows=TR)
        vw = view(Q0, 2, MH * DH, rows=TR)
        cst = view(Q0 + 2 * NT, MH * DH + MH)
        sR = view(Q0 + 1700, MH, SB, rows=NS)
        aLb = view(Q0 + 1732, MH * SB)
        wsb = view(Q0 + 1764, MH, SB, rows=NS)
        s_p = view(XT0, PAGES * PAGE + NS, rows=NS)
        s_pt = view(XT0 + 2080, PAGES + 1, NS)
        XM = Q0
        xm = view(XM, KD, NT)
        WO = MQ0
        wo = view(WO, KD, D)
        SK = XM + KD * NT
        skT = view(SK, 16, NK)
        pqT = view(SK + 2048, 2, NT)
        wpq = [view(W0 + p * 4096, KD, 512) for p in range(2)]
        sc = view(H0, TI, 16, NK, rows=TR)
        TK = MQ0
        sv = view(TK, 16, TOPK, rows=TR)
        siu = view(TK + 256, 16, TOPK, rows=TR).bitcast(U32)
        sif = view(TK + 512, 16, TOPK, rows=TR)
        tks = view(TK + 3584, 4, 256, rows=TR)
        cand = view(TK + 2560, 4, 256, rows=TR)
        cv = view(TK + 1280, PH, TOPK, rows=TR)
        ciu = view(TK + 1408, PH, TOPK, rows=TR).bitcast(U32)
        ca = view(TK + 1536, 2, PH * TOPK, rows=TR)
        cau = view(TK + 1792, 2, PH * TOPK, rows=TR).bitcast(U32)
        pick = view(TK + 2048, 4, PH * TOPK, rows=TR)
        eq = view(TK + 2560, PH, TOPK, TOPK, rows=TR)
        tsum = view(TK + 4608, PH, rows=TR)
        P0 = CO["mask"][0]
        pickT = view(P0, 4, NT)
        ab = view(P0 + 4 * NT, 2, PM)
        hraw = view(P0 + 4 * NT + 2 * PM, 2, PM)
        assert P0 + 4 * NT + 4 * PM <= SMALL

        def sb(name, dims, dt):
            return ctx.enter_context(nc.sbuf_tensor(name, [128] + dims, dt))

        gm1 = sb("gm1", [PM, EC], F32)
        hh, hl = [sb(f"hh{p}", [PM], F32R) for p in range(2)], [sb(f"hl{p}", [PM], F32R) for p in range(2)]
        vraw = [sb(f"vraw{p}", [D], F32) for p in range(2)]
        vh, vl = [sb(f"vh{p}", [D], F32R) for p in range(2)], [sb(f"vl{p}", [D], F32R) for p in range(2)]
        gm = [sb("gm0", [PM, EC], F32), gm1]
        xh, xl = sb("xh", [KD, PM], F32R), sb("xl", [KD, PM], F32R)
        uraw = [sb(f"uraw{p}", [D], F32) for p in range(2)]
        uh, ul = [sb(f"uh{p}", [D], F32R) for p in range(2)], [sb(f"ul{p}", [D], F32R) for p in range(2)]
        oh1 = [sb(f"oh1{p}", [GTM, NK], F32R) for p in range(2)]
        oh2 = [sb(f"oh2{p}", [GTM, 2, EC], F32R) for p in range(2)]
        keys = [sb(f"keys{p}", [GTM], F32) for p in range(2)]
        oheq = sb("oheq", [2, GTM, EC], F32)

        def as32(ap):
            return ap.bitcast(F32)

        yt = gm[0][0:TR].rearrange("p a b -> p (a b)")[:, 0:TI * D].rearrange("p (a b) -> p a b", a=TI)
        lnv2 = gm[1][0:TR].rearrange("p a b -> p (a b)")[:, 0:2 * D].rearrange("p (a b) -> p a b", a=2)

        s = {n: sem(n) for n in (
            "x0_in x_in ident_in consts_in ln_in w_in0 w_in1 wq_in uk_in ct_in nst_in dve_step act_step "
            "var_ready std_ready ln_done ht_ps ht_done z_ps z_done ssq_ready rms_std "
            "tok_done tt_ps tt_done q_ps q_done rot_done qrt_ps qrt_done qrc_ready qrs_ps qs_ready "
            "ls_abs ls_log lf_ready cum_ps dg_ready dg_ps csbc_done "
            "mla_s mla_max mla_exp mla_p mla_tps mla_pt mla_o mla_done "
            "inter_ps numt_done numi_ps inter_done ml_m ml_w ml_qk ml_p ml_tps ml_pt ml_num ml_h hvar hstd ml_gated "
            "mlast_ps ws_lin ws_exp wsp_done vw_ready cst_ps cst_done sel_ready sel_ps sws_lin sws_exp wsb_done "
            "vwb_ready sst_ps sst_done c_in0 c_in1 c_in2 sm_s sm_max sm_exp sm_p sm_tps sm_pt sm_o sm_done "
            "wo_in ln1_in xm_ps xm_done wo_ps res_done pq_in0 pq_in1 sk_in pq_ps pq_done sc_ps sc_done "
            "tk_lin tk_exp tk_pick pk_ps pk_done g_ps g_done u_in0 u_in1 v_in0 v_in1 "
            "s_ps a_done h_done y_ps y_done uh_done ul_done vh_done vl_done xh_done xl_done oh1_ready oh2_ready keys_ready e2_equal h_raw g_high ln2_in yt_ps yt_done pt_in "
            "out_tok out_m out_c out_cs out_y").split()}
        w_in_sem, pq_in, u_in, v_in = ([a, b] for a, b in (
            (s["w_in0"], s["w_in1"]), (s["pq_in0"], s["pq_in1"]), (s["u_in0"], s["u_in1"]), (s["v_in0"], s["v_in1"])))
        c_in = [s["c_in0"], s["c_in1"], s["c_in2"]]
        w, rest = PT[1], 512 - PT[1]
        PIECES = ([(d, 0, PT[0], d // 2, PT[0] * (d % 2)) for d in range(KD)],
                  [(d, 0, w, d, 0) for d in range(5)] + [(5 + n, 0, rest, n, w) for n in range(3)]
                  + [(5 + n, rest, w - rest, 3 + n // 2, w + (w - rest) * (n % 2)) for n in range(3)])
        FIRST = [(i, i * TR // PAIR[0], min((i + 1) * TR // PAIR[0], EC // 2)) for i in range(3)]
        assert TR % PAIR[0] == 0
        NJ = TI * NH

        def tile(i):
            return slice(i * TR, (i + 1) * TR)

        def half(n):
            return slice(n * HALF, (n + 1) * HALF)

        def passes(n):
            return slice(T0[n], T0[n] + PT[n])

        def bc(ap, axis, n):
            return ap.unsqueeze(axis).broadcast_to(ap.shape[:axis] + [n] + ap.shape[axis:]) if isinstance(ap.shape, list) \
                else ap.unsqueeze(axis).broadcast_to(list(ap.shape[:axis]) + [n] + list(ap.shape[axis:]))

        block = ctx.enter_context(nc.Block())

        @block.sync
        def _(sp):
            sp.dma_start(hid[:, 0, :], x[0:TR, :]).then_inc(s["x0_in"], 16)
            sp.dma_start(lnv, lnin[0:TR]).then_inc(s["ln_in"], 16)
            sp.dma_start(ident, consts[:, 0:128]).then_inc(s["ident_in"], 16)
            sp.dma_start(hid[:, 1:TI, :], x[TR:NT, :].rearrange("(i p) d -> p i d", p=TR)).then_inc(s["x_in"], 16)
            for c in range(5):
                if c >= 2:
                    sp.wait_ge(s["z_ps"], TI * (c - 1))
                sp.dma_start(wring[:, c % 2], w_in[c]).then_inc(w_in_sem[c % 2], 16)
                if c == 0:
                    sp.dma_start(lo[:, 128:C_END], consts[:, 128:C_END]).then_inc(s["consts_in"], 16)
                    sp.dma_start(lo[:, C_END:V_END], vecs).then_inc(s["consts_in"], 16)
                    sp.dma_start(ptab[:, :], pages).then_inc(s["pt_in"], 16)
            sp.dma_start(wuk, w_uk).then_inc(s["uk_in"], 16)
            sp.dma_start(wuv, w_uv).then_inc(s["uk_in"], 16)
            sp.wait_ge(s["z_ps"], 4 * TI)
            sp.dma_start(wqb, w_qb).then_inc(s["wq_in"], 16)
            sp.wait_ge(s["tok_done"], 1)
            sp.dma_start(o_ckv.rearrange("(i p) c -> p i c", p=TR), z0[:, :, QR:QR + KVR]).then_inc(s["out_tok"], 16)
            sp.dma_start(o_kpe.rearrange("(i p) c -> p i c", p=TR),
                         z0[:, :, QR + KVR:QR + KVR + ROPE]).then_inc(s["out_tok"], 16)
            sp.wait_ge(s["qs_ready"], 1)
            sp.dma_start(nst, nt0).then_inc(s["nst_in"], 16)
            sp.wait_ge(s["mla_s"], NJ)
            sp.dma_start(ct, ct0).then_inc(s["ct_in"], 16)
            sp.wait_ge(s["cst_done"], 1)
            sp.dma_start(o_c, cst[:, 0:512]).then_inc(s["out_c"], 16)
            sp.dma_start(o_n, cst[:, 512:516]).then_inc(s["out_c"], 16)
            sp.dma_start(o_m.rearrange("(i p) h -> p i h", p=TR), mabs).then_inc(s["out_m"], 16)
            sp.wait_ge(s["sst_done"], SB + 1)
            sp.dma_start(o_cs, ct).then_inc(s["out_cs"], 16)
            sp.dma_start(o_ns, nst).then_inc(s["out_cs"], 16)
            sp.wait_ge(s["pt_in"], 16)
            for b in range(SB):
                if b == 1:
                    sp.wait_ge(s["out_c"], 32)
                    sp.wait_ge(s["out_cs"], 32)
                if b >= 3:
                    sp.wait_ge(s["sm_o"], b - 2)
                with sp.Fori(0, PAGES // 4) as kq:
                    for r in range(4):
                        page = sp.value_load(ptab[0:1, bass.ds(kq * 4 + (b * PAGES + r), 1)], min_val=0, max_val=cache.shape[0] - 1)
                        sp.dma_start(cach[b % 3][:, bass.ds(kq * 4 + r, 1), :].rearrange("p a c -> p (a c)"),
                                     cache[bass.ds(page, 1)].rearrange("a k c -> (a k) c")).then_inc(c_in[b % 3], 16)
            sp.wait_ge(s["sm_done"], SB)
            sp.wait_ge(s["out_tok"], 32)
            sp.dma_start(wo, w_o).then_inc(s["wo_in"], 16)
            sp.dma_start(lnv, ln1[0:TR]).then_inc(s["ln1_in"], 16)
            sp.dma_start(skT, sub_keys).then_inc(s["sk_in"], 16)
            sp.wait_ge(s["xm_done"], 13)
            for c in range(4):
                if c >= 2:
                    sp.wait_ge(s["sc_ps"], 4 * (c - 1))
                sp.dma_start(wpq[c % 2], w_pq[c]).then_inc(pq_in[c % 2], 16)

            def expert_block(p, blk, n):
                if n is not None:
                    sp.wait_ge(s["ul_done"], n)
                sp.dma_start(uraw[p][:, :], eu[blk].rearrange("p k e -> p (k e)")).then_inc(u_in[p], 16)
                if n is not None:
                    sp.wait_ge(s["vl_done"], n)
                sp.dma_start(vraw[p][:, :], ev[blk]).then_inc(v_in[p], 16)

            sp.wait_ge(s["sc_ps"], 16)
            for p in range(2):
                sp.dma_start(uraw[p][:, :], eu[p].rearrange("p k e -> p (k e)")).then_inc(u_in[p], 16)
            sp.wait_ge(s["tk_pick"], TI)
            for p in range(2):
                sp.dma_start(vraw[p][:, :], ev[p]).then_inc(v_in[p], 16)
            for n in range(2):
                if n:
                    for p in range(2):
                        expert_block(p, p, NK + p - 1)
                with sp.Fori(1, NK // 2) as j:
                    for p in range(2):
                        expert_block(p, j * 2 + p, j * 2 + (n * NK + p - 1))
            sp.wait_ge(s["h_done"], 2 * NK)
            sp.dma_start(lnv2, ln2[0:TR]).then_inc(s["ln2_in"], 16)
            for i in range(TI):
                sp.wait_ge(s["ln_done"], 2 * TI + i + 1)
                sp.dma_start(o_y[tile(i), :], yt[:, i, :]).then_inc(s["out_y"], 16)
            sp.wait_ge(s["out_m"], 16)
            sp.wait_ge(s["out_y"], 16 * TI)

        @block.tensor
        def _(pe):
            pe.wait_ge(s["ident_in"], 16)

            def hidden_transposes(n):
                i = n % TI
                pe.wait_ge(s["ln_done"], n + 1)
                if n >= 2:
                    pe.wait_ge(s["ht_done"], n - 1)
                for k in range(KD):
                    last = nc.tensor.transpose(ps[:, 4 + 2 * (n % 2) + k // 4, (k % 4) * TR:(k % 4 + 1) * TR],
                                               hid[:, i, k * 128:(k + 1) * 128], ident[0:TR, 0:TR])
                last.then_inc(s["ht_ps"], 1)

            hidden_transposes(0)
            for g in range(4 * TI + 2 * MH):
                c, i = (g // TI, g % TI) if g < 4 * TI else (4, TI - 1)
                if g + 1 < TI:
                    hidden_transposes(g + 1)
                if i == 0 or g == 4 * TI:
                    pe.wait_ge(w_in_sem[c % 2], 16 * (c // 2 + 1))
                pe.wait_ge(s["ht_done"], i + 1)
                if g >= 4:
                    pe.wait_ge(s["z_done"], g - 3)
                for k in range(KD):
                    if c == 0:
                        last = nc.tensor.matmul(ps[0:TR, g % 4, 0:Z0W], hT[:, k, tile(i)], wring[:, 0, k, 0:Z0W],
                                                start=(k == 0), stop=(k == KD - 1))
                    elif c < 4:
                        last = nc.tensor.matmul(ps[0:TR, g % 4, :], hT[:, k, tile(i)], wring[:, c % 2, k, :],
                                                start=(k == 0), stop=(k == KD - 1))
                    else:
                        h, n = (g - 4 * TI) // 2, g % 2
                        last = nc.tensor.matmul(ps[:, g % 4, 0:HALF], wring[:, 0, k, h * 128:(h + 1) * 128],
                                                hT[:, k, half(n)], start=(k == 0), stop=(k == KD - 1))
                last.then_inc(s["z_ps"], 1)
            pe.wait_ge(s["tok_done"], 1)
            pe.wait_ge(s["ht_done"], TI)
            for i in range(TI):
                if i >= 2:
                    pe.wait_ge(s["tt_done"], i - 1)
                a, b = 4 + 2 * (i % 2), 5 + 2 * (i % 2)
                srcs = [z0[:, i, QR:QR + KVR], kp4[:, i].rearrange("p a r -> p (a r)"), z0[:, i, 0:128], z0[:, i, 128:256]]
                for n, src in enumerate(srcs):
                    nc.tensor.transpose(ps[:, a, n * TR:(n + 1) * TR], src, ident[0:TR, 0:TR])
                for h in range(MH):
                    last = nc.tensor.transpose(ps[:, b, h * TR:(h + 1) * TR], zk[:, i, h * 128:(h + 1) * 128],
                                               ident[0:TR, 0:TR])
                last.then_inc(s["tt_ps"], 1)
            pe.wait_ge(s["wq_in"], 16)
            pe.wait_ge(s["uk_in"], 32)
            pe.wait_ge(s["tt_done"], TI)
            pe.wait_ge(s["z_done"], 28)
            for g in range(29):
                if g >= 4:
                    pe.wait_ge(s["q_done"], g - 3)
                if g < 8:
                    for k in range(2):
                        last = nc.tensor.matmul(ps[:, g % 4, 0:HALF], wqb[:, k, (g // 2) * 128:(g // 2 + 1) * 128],
                                                tt[:, 2 + k, half(g % 2)], start=(k == 0), stop=(k == 1))
                elif g < 13:
                    for k in range(2):
                        last = nc.tensor.matmul(ps[0:TR, g % 4, 0:NH * ROPE], tt[:, 2 + k, tile(g - 8)],
                                                wqb[:, k, 512:768], start=(k == 0), stop=(k == 1))
                else:
                    h, n = (g - 13) // 2, (g - 13) % 2
                    o = 64 * (h % 2)
                    last = nc.tensor.matmul(ps[:, g % 4, 0:HALF], wuk[o:o + 64, h // 2, :], qnT[o:o + 64, h // 2, half(n)],
                                            start=True, stop=True)
                last.then_inc(s["q_ps"], 1)
            for i in range(TI):
                pe.wait_ge(s["rot_done"], i + 1)
                if i >= 2:
                    pe.wait_ge(s["qrt_done"], i - 1)
                for n in range(2):
                    last = nc.tensor.transpose(ps[:, 4 + i % 2, n * TR:(n + 1) * TR], qrk[:, i, n * 128:(n + 1) * 128],
                                               ident[0:TR, 0:TR])
                last.then_inc(s["qrt_ps"], 1)
            pe.wait_ge(s["qrc_ready"], 1)
            for h in range(NH):
                last = nc.tensor.transpose(ps[:, 6, h * NS:(h + 1) * NS], qrc[:, h].rearrange("p a r -> p (a r)"),
                                           ident[0:NS, 0:NS])
            last.then_inc(s["qrs_ps"], 1)
            pe.wait_ge(s["consts_in"], 32)
            pe.wait_ge(s["lf_ready"], 1)
            for t in range(TI):
                for u in range(t + 1):
                    m = const("ltd0" if t == 0 else "ltdc", rows=TR) if u == t else \
                        const("lt01", rows=TR) if u == 0 else ones[0:TR, 0:TR]
                    last = nc.tensor.matmul(ps[0:TR, 7, t * MH:(t + 1) * MH], m, lf[:, u, :], start=(u == 0), stop=(u == t))
            last.then_inc(s["cum_ps"], 1)
            for i in range(TI):
                pe.wait_ge(s["dg_ready"], i + 1)
                if i == 0:
                    pe.wait_ge(s["qrt_done"], TI)
                if i >= 2:
                    pe.wait_ge(s["csbc_done"], i - 1)
                nc.tensor.matmul(ps[:, 4 + i % 2, 0:MH * TR], ones[0:TR, :], dg[:, i % 2].rearrange("p h t -> p (h t)"),
                                 start=True, stop=True).then_inc(s["dg_ps"], 1)
            pe.wait_ge(s["q_done"], 29)
            pe.wait_ge(s["csbc_done"], TI)
            pe.wait_ge(s["qs_ready"], 1)

            def mla_scores(j):
                i, h = divmod(j, NH)
                if j >= 2:
                    pe.wait_ge(s["mla_max"], j - 1)
                o = 32 * (h % 4)
                nk = TR * (i + 1)
                for lo, hi in ((0, min(nk, 512)),) + (((512, nk),) if nk > 512 else ()):
                    out = ps[0:TR, 2 * (j % 2) + lo // 512, 0:hi - lo]
                    nc.tensor.matmul(out, qlT[:, h, tile(i)], tt[:, 0, lo:hi], start=True, stop=False)
                    last = nc.tensor.matmul(out, qrT[o:o + 32, h // 4, tile(i)], tt[o:o + 32, 1, lo:hi],
                                            start=False, stop=True, tile_position=(o, 0))
                last.then_inc(s["mla_s"], 1)

            def turn(src, i):
                for t in range(i + 1):
                    last = nc.tensor.transpose(ps[0:TR, 4 + t // 4, (t % 4) * TR:(t % 4 + 1) * TR], src[:, tile(t)],
                                               ident[0:TR, 0:TR])
                return last

            def mla_turn(j):
                pe.wait_ge(s["mla_p"], j + 1)
                if j >= 1:
                    pe.wait_ge(s["mla_pt"], j)
                turn(sbuf_s[j % 3], j // NH).then_inc(s["mla_tps"], 1)

            def mla_values(j):
                i = j // NH
                pe.wait_ge(s["mla_pt"], j + 1)
                if j >= 2:
                    pe.wait_ge(s["mla_done"], j - 1)
                for t in range(i + 1):
                    last = nc.tensor.matmul(ps[:, 6 + j % 2, 0:TR], z0[:, t, QR:QR + KVR], sbuf_pt[:, j % 2, tile(t)],
                                            start=(t == 0), stop=(t == i))
                last.then_inc(s["mla_o"], 1)

            for j in range(NJ + 3):
                if j < NJ:
                    mla_scores(j)
                if 2 <= j < NJ + 2:
                    mla_turn(j - 2)
                if j >= 3:
                    mla_values(j - 3)
            pe.wait_ge(s["ct_in"], 16)
            pe.wait_ge(s["nst_in"], 16)
            pe.wait_ge(s["mla_done"], NJ)
            for h in range(MH):
                for b in range(SB):
                    nc.tensor.matmul(ps[:, 6, h * NS + 4 * b:h * NS + 4 * b + 4], ct[:, h * SB + b, :],
                                     mqT[:, h, 4 * b:4 * b + 4], start=True, stop=True)
            for h in range(MH):
                last = nc.tensor.matmul(ps[0:NS, 6, 256 + h * SB:256 + (h + 1) * SB], mqT[:, h, 0:NS], nst[:, h, :],
                                        start=True, stop=True)
            last.then_inc(s["inter_ps"], 1)
            pe.wait_ge(s["numt_done"], 1)
            for h in range(MH):
                last = nc.tensor.transpose(ps[0:NS, 7, h * 128:(h + 1) * 128], numT[:, h, :], ident)
            last.then_inc(s["numi_ps"], 1)
            pe.wait_ge(s["inter_done"], 1)

            def ml_scores(n):
                i, h = divmod(n, MH)
                if n >= 2:
                    pe.wait_ge(s["ml_p"], n - 1)
                nk = TR * (i + 1)
                for lo, hi in ((0, min(nk, 512)),) + (((512, nk),) if nk > 512 else ()):
                    last = nc.tensor.matmul(ps[0:TR, 2 * (n % 2) + lo // 512, 0:hi - lo], mqT[:, h, tile(i)],
                                            tt[:, 4 + h, lo:hi], start=True, stop=True)
                last.then_inc(s["ml_qk"], 1)

            def ml_turn(n):
                i, h = divmod(n, MH)
                pe.wait_ge(s["ml_p"], n + 1)
                if n >= 1:
                    pe.wait_ge(s["ml_pt"], n)
                turn(wexp[:, h], i).then_inc(s["ml_tps"], 1)

            def ml_values(n):
                i, h = divmod(n, MH)
                pe.wait_ge(s["ml_pt"], n + 1)
                if i >= 1 and h == 0:
                    pe.wait_ge(s["ml_h"], i)
                for t in range(i + 1):
                    last = nc.tensor.matmul(ps[0:TR, 6, h * 128:(h + 1) * 128], sbuf_pt[:, n % 2, tile(t)],
                                            zv[:, t, h * 128:(h + 1) * 128], start=(t == 0), stop=(t == i))
                last.then_inc(s["ml_num"], 1)

            for i in range(TI):
                for h in range(MH + 2):
                    n = i * MH + h
                    if h < MH:
                        ml_scores(n)
                    if 1 <= h <= MH:
                        ml_turn(n - 1)
                    if h >= 2:
                        ml_values(n - 2)
            nc.tensor.matmul(ps[:, 7, 0:MH], const("sellast", rows=TR), mm[:, TI - 1, :], start=True, stop=True)
            nc.tensor.matmul(ps[0:NS, 7, 8:8 + MH], const("lsel", rows=NS), mm[0:NS, 0, :],
                             start=True, stop=True).then_inc(s["mlast_ps"], 1)
            pe.wait_ge(s["wsp_done"], 1)
            for i in range(TI):
                pe.wait_ge(s["vw_ready"], i + 1)
                for h in range(MH):
                    k = zk[:, i, h * 128:(h + 1) * 128]
                    nc.tensor.matmul(ps[:, 0, h * 128:(h + 1) * 128], k, vw[:, i % 2, h * 128:(h + 1) * 128],
                                     start=(i == 0 and h == 0), stop=(i == TI - 1), skip_group_check=True)
                    last = nc.tensor.matmul(ps[:, 1, h:h + 1], k, wsp[:, i, h:h + 1],
                                            start=(i == 0 and h == 0), stop=(i == TI - 1), skip_group_check=True)
                last.then_inc(s["cst_ps"], 1)
            pe.wait_ge(s["sel_ready"], 1)
            nc.tensor.matmul(ps[:, 7, 16:48], ones[0:NS, :], sR.rearrange("p h b -> p (h b)"),
                             start=True, stop=True).then_inc(s["sel_ps"], 1)
            pe.wait_ge(s["wsb_done"], 1)
            for h in range(MH):
                last = nc.tensor.matmul(ps[:, 6, h * SB:(h + 1) * SB], zk[0:NS, 0, h * 128:(h + 1) * 128], wsb[:, h, :],
                                        start=True, stop=True)
            last.then_inc(s["sst_ps"], 1)
            for b in range(SB):
                pe.wait_ge(s["vwb_ready"], b + 1)
                if b >= 2:
                    pe.wait_ge(s["sst_done"], b)
                for h in range(MH):
                    last = nc.tensor.matmul(ps[:, 2 + b % 2, h * 128:(h + 1) * 128], zk[0:NS, 0, h * 128:(h + 1) * 128],
                                            vw[0:NS, b % 2, h * 128:(h + 1) * 128], start=True, stop=True)
                last.then_inc(s["sst_ps"], 1)
            pe.wait_ge(s["sst_done"], SB + 1)
            pe.wait_ge(s["cst_done"], 1)

            def sm_scores(b):
                page = cach[b % 3]
                pe.wait_ge(c_in[b % 3], 16 * PAGES * (b // 3 + 1))
                if b >= 1:
                    pe.wait_ge(s["sm_max"], b)
                    pe.wait_ge(s["sm_exp"], b)
                for q in range(4):
                    nc.tensor.matmul(ps[0:NS, q, :], qs[:, b, :], page[:, :, KVR + 32 * q:KVR + 32 * q + 32],
                                     start=True, stop=False)
                    nc.tensor.matmul(ps[0:NS, q, :], qrs4[32 * q:32 * q + 32, b, :], page[32 * q:32 * q + 32, :, KVR + PAGE:RECORD],
                                     start=False, stop=True, tile_position=(32 * q, 0))
                nc.tensor.matmul(ps[0:NS, 4, 0:NS], qs[:, b, :], tt[:, 0, 0:NS], start=True, stop=False)
                nc.tensor.matmul(ps[0:NS, 4, 0:NS], qrs4[0:32, b, :], tt[0:32, 1, 0:NS],
                                 start=False, stop=True, tile_position=(0, 0)).then_inc(s["sm_s"], 1)

            sm_scores(0)
            for b in range(SB):
                if b + 1 < SB:
                    sm_scores(b + 1)
                pe.wait_ge(s["sm_p"], b + 1)
                for k in range(PAGES):
                    nc.tensor.transpose(ps[:, 5, k * NS:(k + 1) * NS], s_p[:, k * 128:(k + 1) * 128], ident[0:NS, 0:NS])
                nc.tensor.transpose(ps[0:NS, 6, 0:NS], s_p[:, 2048:2048 + NS], ident[0:NS, 0:NS]).then_inc(s["sm_tps"], 1)
                pe.wait_ge(s["sm_pt"], b + 1)
                if b >= 1:
                    pe.wait_ge(s["sm_done"], b)
                for k in range(PAGES):
                    nc.tensor.matmul(ps[:, 7, 0:NS], cach[b % 3][:, k, 0:KVR], s_pt[:, k, :], start=(k == 0), stop=False)
                nc.tensor.matmul(ps[:, 7, 0:NS], z0[0:NS, 0, QR:QR + KVR], s_pt[0:NS, PAGES, :],
                                 start=False, stop=True).then_inc(s["sm_o"], 1)
            pe.wait_ge(s["sm_done"], SB)
            for g in range(8):
                if g >= 4:
                    pe.wait_ge(s["xm_done"], g - 3)
                for h in (2 * (g // 2), 2 * (g // 2) + 1):
                    o = 64 * (h % 2)
                    last = nc.tensor.matmul(ps[o:o + 64, g % 4, 0:HALF], wuv[:, h * VD:(h + 1) * VD], olT[:, h, half(g % 2)],
                                            start=True, stop=True)
                last.then_inc(s["xm_ps"], 1)
            pe.wait_ge(s["ml_gated"], TI)
            for i in range(TI):
                pe.wait_ge(s["xm_done"], 5 + i)
                for h in range(MH):
                    last = nc.tensor.transpose(ps[:, (8 + i) % 4, h * TR:(h + 1) * TR], zo[:, i, h * 128:(h + 1) * 128],
                                               ident[0:TR, 0:TR])
                last.then_inc(s["xm_ps"], 1)
            pe.wait_ge(s["wo_in"], 16)
            pe.wait_ge(s["xm_done"], 13)
            for g in range(2 * TI):
                if g >= 4:
                    pe.wait_ge(s["res_done"], g - 3)
                for k in range(KD):
                    last = nc.tensor.matmul(ps[0:TR, g % 4, :], xm[:, k, tile(g // 2)],
                                            wo[:, k, (g % 2) * 512:(g % 2 + 1) * 512], start=(k == 0), stop=(k == KD - 1))
                last.then_inc(s["wo_ps"], 1)
                if g % 2 and g > 1:
                    hidden_transposes(TI + g // 2 - 1)
            hidden_transposes(2 * TI - 1)
            pe.wait_ge(s["ht_done"], 2 * TI)
            pe.wait_ge(s["res_done"], 2 * TI)
            pe.wait_ge(s["sk_in"], 16)
            for hp in range(2 * PH):
                c = hp // 4
                pe.wait_ge(pq_in[c % 2], 16 * (c // 2 + 1))
                for n in range(2):
                    if 2 * hp + n >= 4:
                        pe.wait_ge(s["pq_done"], 2 * hp + n - 3)
                    for k in range(KD):
                        last = nc.tensor.matmul(ps[:, (2 * hp + n) % 4, 0:HALF], wpq[c % 2][:, k, (hp % 4) * 128:(hp % 4 + 1) * 128],
                                                hT[:, k, half(n)], start=(k == 0), stop=(k == KD - 1))
                    last.then_inc(s["pq_ps"], 1)
                pe.wait_ge(s["pq_done"], 2 * hp + 2)
                if hp >= 2:
                    pe.wait_ge(s["sc_done"], hp - 1)
                for i in range(TI):
                    last = nc.tensor.matmul(ps[0:TR, 4 + 2 * (hp % 2) + i // 4, (i % 4) * 128:(i % 4 + 1) * 128],
                                            pqT[:, hp % 2, tile(i)], skT[:, hp, :], start=True, stop=True)
                last.then_inc(s["sc_ps"], 1)
            def gates(p, g, n, n_free):
                pe.wait_ge(s["oh1_ready"], g)
                pe.wait_ge(s["oh2_ready"], g)
                if n_free is not None:
                    pe.wait_ge(s["g_done"], n_free)
                for t in range(GTS[n][p]):
                    last = nc.tensor.matmul(ps[:, 6 + t // 8, (t % 8) * 2 * EC:(t % 8 + 1) * 2 * EC], oh1[p][:, t, :],
                                            oh2[p][:, t].rearrange("p a e -> p (a e)"), start=True, stop=True)
                last.then_inc(s["g_ps"], 1)

            def up(p, n, n_u, n_free):
                pe.wait_ge(s["ul_done"], n_u)
                if n_free is not None:
                    pe.wait_ge(s["a_done"], n_free)
                for k in range(KD):
                    for a, b in ((uh, xh), (uh, xl), (ul, xh)):
                        last = nc.tensor.matmul(ps[:, 5, 0:PT[n]], a[p][:, k * 128:(k + 1) * 128], b[:, k, 0:PT[n]],
                                                start=(k == 0 and b is xh and a is uh), stop=(k == KD - 1 and a is ul))
                last.then_inc(s["s_ps"], 1)

            def down(p, n, n_h, first, last_block):
                pe.wait_ge(s["h_done"], n_h)
                pe.wait_ge(s["vl_done"], n_h)
                for a, b in ((vh, hh), (vh, hl), (vl, hh)):
                    for d, t0, m, bank, col in PIECES[n]:
                        last = nc.tensor.matmul(ps[:, bank, col:col + m], a[p][:, d * 128:(d + 1) * 128], b[p][:, t0:t0 + m],
                                                start=(first and col == 0 and a is vh and b is hh),
                                                stop=(last_block and a is vl), skip_group_check=True)
                last.then_inc(s["y_ps"], 1)

            pe.wait_ge(s["sc_done"], 16)
            for i in range(TI):
                pe.wait_ge(s["tk_pick"], i + 1)
                if i >= 2:
                    pe.wait_ge(s["pk_done"], i - 1)
                for n in range(4):
                    last = nc.tensor.transpose(ps[:, i % 2, n * TR:(n + 1) * TR], pick[:, n, :], ident[0:TR, 0:TR])
                last.then_inc(s["pk_ps"], 1)
                if i < len(FIRST):
                    for g in range(2 * FIRST[i][1], 2 * FIRST[i][2]):
                        gates(g % 2, g + 1, 0, g or None)
            pe.wait_ge(s["pk_done"], TI)
            for n in range(2):
                pe.wait_ge(s["xl_done"], n + 1)
                if n == 1:
                    pe.wait_ge(s["y_done"], 1)
                up(0, n, n * NK + 1, n * NK if n else None)
                for r in range(ROUNDS * n, ROUNDS * (n + 1)):
                    b0 = r * EC

                    def pair(j, first=False, last=False):
                        for p in range(2):
                            if r < 2 * ROUNDS - 1:
                                gates(p, j * 2 + (b0 + EC + p + 1), (r + 1) // ROUNDS, j * 2 + (b0 + EC + p))
                            if not (last and p == 1):
                                up(1 - p, n, j * 2 + (b0 + p + 2), j * 2 + (b0 + p + 1))
                            down(p, n, j * 2 + (b0 + p + 1), first and p == 0, last and p == 1)

                    start, end = int(r % ROUNDS == 0), EC // 2 - int(r % ROUNDS == ROUNDS - 1)
                    if start:
                        pair(0, first=True)
                    with pe.Fori(start, end) as j:
                        pair(j)
                    if end < EC // 2:
                        pair(EC // 2 - 1, last=True)
            pe.wait_ge(s["y_done"], 2)
            for i in range(TI):
                if i >= 2:
                    pe.wait_ge(s["yt_done"], i - 1)
                for k in range(KD):
                    last = nc.tensor.transpose(ps[0:TR, 2 * (i % 2) + k // 4, (k % 4) * 128:(k % 4 + 1) * 128],
                                               hT[:, k, tile(i)], ident)
                last.then_inc(s["yt_ps"], 1)

        @block.scalar
        def _(act):
            steps = [0]

            def step(ins):
                steps[0] += 1
                ins.then_inc(s["act_step"], 1)
                act.wait_ge(s["act_step"], steps[0])

            def copy(out, in_):
                return nc.scalar.activation(out, in_, ACT.Copy)

            def norm_roots(at):
                for i in range(TI):
                    act.wait_ge(s["var_ready"], at + i + 1)
                    nc.scalar.activation(rstd[:, i:i + 1], rs1, ACT.Sqrt).then_inc(s["std_ready"], 1)
                    if at < 2 * TI and i >= 1:
                        hidden_copies(at + i - 1)
                    if at == 2 * TI and i + 2 < TI:
                        y_copy(i + 2)
                if at < 2 * TI:
                    hidden_copies(at + TI - 1)

            def y_copy(i):
                act.wait_ge(s["yt_ps"], i + 1)
                b = 2 * (i % 2)
                copy(yt[:, i, :].rearrange("p (a b) -> p a b", a=2), ps[0:TR, b:b + 2, :]).then_inc(s["yt_done"], 1)

            def hidden_copies(n):
                i = n % TI
                act.wait_ge(s["ht_ps"], n + 1)
                for a in range(2):
                    last = copy(hT[:, 4 * a:4 * a + 4, tile(i)],
                                ps[:, 4 + 2 * (n % 2) + a, 0:4 * TR].rearrange("p (k t) -> p k t", k=4))
                last.then_inc(s["ht_done"], 1)

            norm_roots(0)
            for g in range(28):
                act.wait_ge(s["z_ps"], g + 1)
                c, i = g // TI, g % TI
                if c == 0:
                    ins = copy(z0[:, i, :], ps[0:TR, g % 4, 0:Z0W])
                elif c == 1:
                    ins = nc.scalar.activation(zk[:, i, :], ps[0:TR, g % 4, :], ACT.Copy, scale=float(DH ** -0.5))
                elif c == 2:
                    ins = copy(zv[:, i, :], ps[0:TR, g % 4, :])
                elif c == 3:
                    ins = nc.scalar.activation(zo[:, i, :], ps[0:TR, g % 4, :], ACT.Sigmoid)
                else:
                    ins = copy(mqT[:, (g - 20) // 2, half(g % 2)], ps[:, g % 4, 0:HALF])
                ins.then_inc(s["z_done"], 1)
            act.wait_ge(s["ssq_ready"], 1)
            nc.scalar.activation(ssq, ssq, ACT.Sqrt).then_inc(s["rms_std"], 1)
            for i in range(TI):
                act.wait_ge(s["tt_ps"], i + 1)
                for a in range(2):
                    last = copy(tt[:, 4 * a:4 * a + 4, tile(i)],
                                ps[:, 4 + 2 * (i % 2) + a, 0:4 * TR].rearrange("p (k t) -> p k t", k=4))
                last.then_inc(s["tt_done"], 1)
            for g in range(29):
                act.wait_ge(s["q_ps"], g + 1)
                if g < 8:
                    ins = copy(qnT[:, g // 2, half(g % 2)], ps[:, g % 4, 0:HALF])
                elif g < 13:
                    ins = copy(qrk[:, g - 8, :], ps[0:TR, g % 4, 0:NH * ROPE])
                else:
                    ins = copy(qlT[:, (g - 13) // 2, half((g - 13) % 2)], ps[:, g % 4, 0:HALF])
                ins.then_inc(s["q_done"], 1)
            for i in range(TI):
                act.wait_ge(s["qrt_ps"], i + 1)
                copy(qrT[:, :, tile(i)], ps[:, 4 + i % 2, 0:2 * TR].rearrange("p (k t) -> p k t", k=2)).then_inc(s["qrt_done"], 1)
            act.wait_ge(s["ls_abs"], 1)
            step(nc.scalar.activation(glog, gabs, ACT.Exp, scale=-1.0))
            nc.scalar.activation(glog, glog, ACT.Ln, bias=1.0).then_inc(s["ls_log"], 1)
            for i in range(TI):
                act.wait_ge(s["dg_ps"], i + 1)
                copy(cs_bc[:, :, tile(i)], ps[:, 4 + i % 2, 0:MH * TR].rearrange("p (h t) -> p h t", h=MH))\
                    .then_inc(s["csbc_done"], 1)

            def pt_copy(i, par):
                n = min(i + 1, 4) * TR
                last = copy(sbuf_pt[:, par, 0:n], ps[0:TR, 4, 0:n])
                if i == 4:
                    last = copy(sbuf_pt[:, par, n:n + TR], ps[0:TR, 5, 0:TR])
                return last

            def mla_pt(j):
                act.wait_ge(s["mla_tps"], j + 1)
                if j >= 2:
                    act.wait_ge(s["mla_o"], j - 1)
                pt_copy(j // NH, j % 2).then_inc(s["mla_pt"], 1)

            for j in range(NJ + 2):
                if j < NJ:
                    act.wait_ge(s["mla_max"], j + 1)
                    nk = TR * (j // NH + 1)
                    nc.scalar.activation(sbuf_s[j % 3][:, 0:nk], sbuf_s[j % 3][:, 0:nk], ACT.Exp, bias=nb[:, j % 3],
                                         scale=SM_SCALE, accum_out=rsum[:, j % 3]).then_inc(s["mla_exp"], 1)
                if j >= 2:
                    mla_pt(j - 2)

            def ml_pt(n):
                act.wait_ge(s["ml_tps"], n + 1)
                if n >= 2:
                    act.wait_ge(s["ml_num"], n - 1)
                pt_copy(n // MH, n % 2).then_inc(s["ml_pt"], 1)

            for i in range(TI):
                nk = TR * (i + 1)
                act.wait_ge(s["ml_m"], i + 1)
                for h in range(MH):
                    nc.scalar.activation(wexp[:, h, 0:nk], wexp[:, h, 0:nk], ACT.Exp, bias=nm[:, i, h:h + 1]).then_inc(s["ml_w"], 1)
                nc.scalar.activation(emm[:, i, :], mabs[:, i, :], ACT.Exp, scale=-1.0)
                nc.scalar.activation(am[:, i, :], am[:, i, :], ACT.Exp).then_inc(s["ml_w"], 1)
                for h in range(MH):
                    ml_pt(i * MH + h)
                act.wait_ge(s["hvar"], i + 1)
                nc.scalar.activation(rs4, rs4, ACT.Sqrt).then_inc(s["hstd"], 1)
            act.wait_ge(s["ws_lin"], 1)
            nc.scalar.activation(wsp, wsp, ACT.Exp).then_inc(s["ws_exp"], 1)
            act.wait_ge(s["sws_lin"], 1)
            nc.scalar.activation(wss, wss, ACT.Exp).then_inc(s["sws_exp"], 1)
            for b in range(SB):
                act.wait_ge(s["sm_max"], b + 1)
                if b >= 1:
                    act.wait_ge(s["sm_tps"], b)
                step(nc.scalar.activation(s_p[:, 0:2048].rearrange("p (g q k) -> p q g k", g=PAGES, q=4),
                                          ps[0:NS, 0:4, :].rearrange("p q (g k) -> p q g k", g=PAGES), ACT.Exp,
                                          bias=smx[:, 2:3], scale=SM_SCALE, accum_out=smx[:, 0:1]))
                nc.scalar.activation(s_p[:, 2048:2080], s_p[:, 2048:2080], ACT.Exp, bias=smx[:, 2:3], scale=SM_SCALE,
                                     accum_out=smx[:, 1:2]).then_inc(s["sm_exp"], 1)
                act.wait_ge(s["sm_tps"], b + 1)
                if b >= 1:
                    act.wait_ge(s["sm_o"], b)
                copy(s_pt[:, 0:PAGES, :], ps[:, 5, :].rearrange("p (k q) -> p k q", k=PAGES))
                copy(s_pt[0:NS, PAGES, :], ps[0:NS, 6, 0:NS]).then_inc(s["sm_pt"], 1)
            for g in range(13):
                act.wait_ge(s["xm_ps"], g + 1)
                if g < 8:
                    ins = copy(xm[:, g // 2, half(g % 2)], ps[:, g % 4, 0:HALF])
                else:
                    ins = copy(xm[:, 4:8, tile(g - 8)], ps[:, g % 4, 0:MH * TR].rearrange("p (h t) -> p h t", h=MH))
                ins.then_inc(s["xm_done"], 1)
            norm_roots(TI)
            for hp in range(2 * PH):
                if hp >= 2:
                    act.wait_ge(s["sc_ps"], hp - 1)
                for n in range(2):
                    act.wait_ge(s["pq_ps"], 2 * hp + n + 1)
                    copy(pqT[:, hp % 2, half(n)], ps[:, (2 * hp + n) % 4, 0:HALF]).then_inc(s["pq_done"], 1)
            def gate_high(p, tok, r, n):
                m = GTS[r // ROUNDS][p]
                act.wait_ge(s["g_ps"], n)
                g = ps[:, 6:8, :].rearrange("p b c -> p (b c)")[:, 0:m * 2 * EC].rearrange("p (t a e) -> p t a e", t=m, a=2)
                copy(gm[r % 2][:, bass.ds(tok, m), :], g[:, :, 0]).then_inc(s["g_high"], 1)

            def high_part(dst, src, sem_in, n_in, free, n_free, done):
                act.wait_ge(sem_in, n_in)
                if n_free is not None:
                    act.wait_ge(free, n_free)
                copy(dst[:, :], src[:, :]).then_inc(done, 1)

            def gelu(p, n, n_s, n_free):
                act.wait_ge(s["s_ps"], n_s)
                if n_free is not None:
                    act.wait_ge(s["h_done"], n_free)
                nc.scalar.activation(ab[:, p, 0:PT[n]], ps[:, 5, 0:PT[n]], ACT.Gelu_apprx_tanh).then_inc(s["a_done"], 1)

            act.wait_ge(s["ht_done"], 2 * TI)
            act.wait_ge(s["sc_ps"], 16)
            copy(xh[:, :, 0:PT[0]], hT[:, :, passes(0)]).then_inc(s["xh_done"], 1)
            for p in range(2):
                high_part(uh[p], uraw[p], u_in[p], 16, None, None, s["uh_done"])
            for i in range(TI):
                act.wait_ge(s["tk_lin"], i + 1)
                nc.scalar.activation(cv, cv, ACT.Exp).then_inc(s["tk_exp"], 1)
                act.wait_ge(s["pk_ps"], i + 1)
                copy(pickT[:, :, tile(i)], ps[:, i % 2, 0:4 * TR].rearrange("p (k t) -> p k t", k=4)).then_inc(s["pk_done"], 1)
                if i < len(FIRST):
                    for g in range(2 * FIRST[i][1], 2 * FIRST[i][2]):
                        gate_high(g % 2, g * GTS[0][0], 0, g + 1)
            high_part(vh[0], vraw[0], v_in[0], 16, None, None, s["vh_done"])
            for r in range(2 * ROUNDS):
                n, b0 = r // ROUNDS, r * EC
                if r == ROUNDS:
                    act.wait_ge(s["s_ps"], NK)
                    copy(xh[:, :, 0:PT[1]], hT[:, :, passes(1)]).then_inc(s["xh_done"], 1)

                if r >= 1:
                    act.wait_ge(s["h_done"], b0)

                def next_gates(j, p):
                    m = (r + 1) // ROUNDS
                    if r < 2 * ROUNDS - 1:
                        gate_high(p, j * PAIR[m] + p * GTS[m][0], r + 1, j * 2 + (b0 + EC + p + 1))

                def block(j, p, n_free, last):
                    gelu(p, n, j * 2 + (b0 + p + 1), n_free)
                    if last < 2:
                        high_part(uh[p], uraw[p], u_in[p], j * 16 + (b0 * 8 + 32), s["s_ps"], j * 2 + (b0 + p + 1), s["uh_done"])
                    if last < 3:
                        high_part(vh[1 - p], vraw[1 - p], v_in[1 - p], j * 16 + (b0 * 8 + 16 + 16 * p), s["y_ps"],
                                  j * 2 + (b0 + p) if n_free is not None else None, s["vh_done"])
                    next_gates(j, p)

                start, end = int(r == 0), EC // 2 - int(r == 2 * ROUNDS - 1)
                if start:
                    block(0, 0, None, 0)
                    act.wait_ge(s["y_ps"], 1)
                    gelu(1, 0, 2, None)
                    high_part(uh[1], uraw[1], u_in[1], 32, s["s_ps"], 2, s["uh_done"])
                    high_part(vh[0], vraw[0], v_in[0], 32, s["y_ps"], 1, s["vh_done"])
                    next_gates(0, 1)
                with act.Fori(start, end) as j:
                    for p in range(2):
                        block(j, p, j * 2 + (b0 + p - 1), 0)
                if end < EC // 2:
                    for p in range(2):
                        block(end, p, b0 + EC - 3 + p, 2 + p)
            for i in range(2):
                y_copy(i)
            norm_roots(2 * TI)

        @block.gpsimd
        def _(pool):
            def first_keys(tok, n, g):
                if g > 1:
                    pool.wait_ge(s["oh1_ready"], g - 1)
                nc.gpsimd.tensor_copy(keys[0][:, 0:GTS[n][0]], pickT[:, 0, tok:tok + GTS[n][0]]).then_inc(s["keys_ready"], 1)

            def key_rows(p, n, tok, g, first=False, last=False):
                if not first:
                    pool.wait_ge(s["g_ps"], g + -2)
                if not (first and p == 0):
                    pool.wait_ge(s["oh1_ready"], g + -1)
                pool.wait_ge(s["keys_ready"], g)
                if not last:
                    m = GTS[n][1 - p]
                    nc.gpsimd.tensor_copy(keys[1 - p][:, 0:m], pickT[:, 0, bass.ds(tok, m)]).then_inc(s["keys_ready"], 1)
                for t in range(GTS[n][p]):
                    ins = nc.gpsimd.tensor_scalar(oh1[p][:, t, :], iota, keys[p][:, t:t + 1], None, ALU.is_equal)
                ins.then_inc(s["oh1_ready"], 1)

            def stretch(n, t0, g0, pairs):
                first_keys(t0, n, g0 + 1)
                a = GTS[n][0]
                if g0 == 0:
                    for p in range(2):
                        key_rows(p, n, (p + 1) * a, p + 1, first=True)
                with pool.Fori(int(g0 == 0), pairs - 1) as j:
                    for p in range(2):
                        key_rows(p, n, j * PAIR[n] + (t0 + (PAIR[n] if p else a)), j * 2 + (g0 + p + 1))
                for p in range(2):
                    key_rows(p, n, t0 + (pairs - 1) * PAIR[n] + a, g0 + 2 * pairs - 1 + p, last=(p == 1))

            for i, a, b in FIRST:
                pool.wait_ge(s["pk_done"], i + 1)
                stretch(0, a * PAIR[0], 2 * a, b - a)
            pool.wait_ge(s["pk_done"], TI)
            for r in range(1, 2 * ROUNDS):
                stretch(r // ROUNDS, T0[r // ROUNDS], r * EC, EC // 2)

        @block.vector
        def _(dve):
            steps = [0]
            v = nc.vector

            def step(ins):
                steps[0] += 1
                ins.then_inc(s["dve_step"], 1)
                dve.wait_ge(s["dve_step"], steps[0])

            def layer_norm(row, i, n, g, b):
                for a in range(2):
                    ins = v.bn_stats(st6[:, a, :], row[:, a * 512:(a + 1) * 512])
                step(ins)
                step(v.bn_aggr(mv2, st6[:, 0:2, :]))
                v.tensor_scalar(rs1, mv2[:, 1:2], 1e-5, None, ALU.add).then_inc(s["var_ready"], 1)
                v.scalar_tensor_tensor(row, row, mv2[:, 0:1], g, ALU.subtract, ALU.mult)
                dve.wait_ge(s["std_ready"], n + 1)
                step(v.reciprocal(rstd[:, i:i + 1], rstd[:, i:i + 1]))
                v.scalar_tensor_tensor(row, row, rstd[:, i:i + 1], b, ALU.mult, ALU.add).then_inc(s["ln_done"], 1)

            dve.wait_ge(s["x0_in"], 16)
            dve.wait_ge(s["ln_in"], 16)
            for i in range(TI):
                if i == 1:
                    dve.wait_ge(s["x_in"], 16)
                layer_norm(hid[:, i, :], i, i, lnv[:, 0, :], lnv[:, 1, :])
            dve.wait_ge(s["consts_in"], 32)
            dve.wait_ge(s["z_done"], TI)
            for i in range(TI):
                ckv, cq = z0[:, i, QR:QR + KVR], z0[:, i, 0:QR]
                v.tensor_tensor_reduce(junk[:, 0:KVR], ckv, ckv, 1.0, 0.0, ALU.mult, ALU.add, ssq[:, i, 0:1])
                step(v.tensor_tensor_reduce(junk[:, 256:512], cq, cq, 1.0, 0.0, ALU.mult, ALU.add, ssq[:, i, 1:2]))
            v.tensor_scalar(ssq[:, :, 0], ssq[:, :, 0], 1.0 / KVR, 1e-6, ALU.mult, ALU.add)
            v.tensor_scalar(ssq[:, :, 1], ssq[:, :, 1], 1.0 / QR, 1e-6, ALU.mult, ALU.add).then_inc(s["ssq_ready"], 1)
            x1, x2 = z0[:, :, QR + KVR:QR + KVR + 16], z0[:, :, QR + KVR + 16:QR + KVR + 32]
            t4 = [rtmp[:, n].rearrange("p (i r) -> p i r", i=TI) for n in range(4)]
            v.tensor_tensor(t4[0], x1, cos, ALU.mult)
            v.tensor_tensor(t4[1], x2, sin, ALU.mult)
            v.tensor_tensor(t4[2], x1, sin, ALU.mult)
            step(v.tensor_tensor(t4[3], x2, cos, ALU.mult))
            v.tensor_tensor(x1, t4[0], t4[1], ALU.subtract)
            step(v.tensor_tensor(x2, t4[2], t4[3], ALU.add))
            for c in range(4):
                v.tensor_copy(kp4[:, :, c, :], z0[:, :, QR + KVR:QR + KVR + ROPE])
            dve.wait_ge(s["rms_std"], 1)
            step(v.reciprocal(ssq, ssq))
            for i in range(TI):
                ckv, cq = z0[:, i, QR:QR + KVR], z0[:, i, 0:QR]
                v.scalar_tensor_tensor(ckv, ckv, ssq[:, i, 0:1], const("kvg", rows=TR), ALU.mult, ALU.mult)
                ins = v.scalar_tensor_tensor(cq, cq, ssq[:, i, 1:2], const("qg", rows=TR), ALU.mult, ALU.mult)
            ins.then_inc(s["tok_done"], 1)
            dve.wait_ge(s["q_done"], 13)
            dve.wait_ge(s["ln_done"], TI)
            for i in range(TI):
                qv = qrk[:, i, :].rearrange("p (h r) -> p h r", h=NH)
                a, b = qv[:, :, 0:16], qv[:, :, 16:32]
                ci, si = bc(cos[:, i, :], 1, NH), bc(sin[:, i, :], 1, NH)
                v.tensor_tensor(rqt[:, 0], a, ci, ALU.mult)
                v.tensor_tensor(rqt[:, 1], b, si, ALU.mult)
                v.tensor_tensor(rqt[:, 2], a, si, ALU.mult)
                step(v.tensor_tensor(rqt[:, 3], b, ci, ALU.mult))
                v.tensor_tensor(a, rqt[:, 0], rqt[:, 1], ALU.subtract)
                ins = v.tensor_tensor(b, rqt[:, 2], rqt[:, 3], ALU.add)
                ins.then_inc(s["rot_done"], 1)
                dve.wait_ge(s["rot_done"], i + 1)
            q0 = qrk[0:NS, 0, :].rearrange("p (h r) -> p h r", h=NH)
            for c in range(4):
                ins = v.tensor_copy(qrc[:, :, c, :], q0)
            ins.then_inc(s["qrc_ready"], 1)
            dve.wait_ge(s["q_done"], 29)
            v.tensor_copy(qs.rearrange("p b (h t) -> p b h t", h=NH),
                          qlT[:, :, 0:NS].rearrange("p h (b t) -> p b h t", b=SB))
            dve.wait_ge(s["qrs_ps"], 1)
            v.tensor_copy(qrs4.rearrange("p b (h t) -> p b h t", h=NH),
                          ps[:, 6, 0:256].rearrange("p (h b t) -> p b h t", h=NH, b=SB)).then_inc(s["qs_ready"], 1)
            step(v.tensor_tensor(gat, z0[:, :, QR + KVR + ROPE:Z0W], bc(const("bg", rows=TR), 1, TI), ALU.add))
            v.scalar_tensor_tensor(gabs, gat[:, :, MH:2 * MH], -1.0, gat[:, :, MH:2 * MH], ALU.mult, ALU.max).then_inc(s["ls_abs"], 1)
            step(v.tensor_scalar(lf, gat[:, :, MH:2 * MH], 0.0, None, ALU.min))
            dve.wait_ge(s["ls_log"], 1)
            v.tensor_tensor(lf, lf, glog, ALU.subtract).then_inc(s["lf_ready"], 1)
            dve.wait_ge(s["cum_ps"], 1)
            step(v.tensor_copy(cum, ps[0:TR, 7, 0:TI * MH].rearrange("p (i h) -> p i h", i=TI)))
            step(v.tensor_tensor(cs, gat[:, :, 0:MH], cum, ALU.subtract))
            dve.wait_ge(s["z_ps"], 28)
            for i in range(TI):
                if i >= 2:
                    dve.wait_ge(s["dg_ps"], i - 1)
                v.tensor_tensor(dg[:, i % 2], bc(ident[0:TR, 0:TR], 1, MH), bc(cs[:, i, :], 2, TR), ALU.mult)\
                    .then_inc(s["dg_ready"], 1)

            def mla_max(j):
                nk = TR * (j // NH + 1)
                dve.wait_ge(s["mla_s"], j + 1)
                if j >= 3:
                    dve.wait_ge(s["mla_tps"], j - 2)
                src = ps[0:TR, 2 * (j % 2):2 * (j % 2) + 2, :].rearrange("p a b -> p (a b)")[:, 0:nk]
                step(v.tensor_tensor_reduce(sbuf_s[j % 3][:, 0:nk], src, mask[:, j // NH, 0:nk], 1.0, -3e38,
                                            ALU.add, ALU.max, mx1[:, j % 3]))
                v.tensor_scalar(nb[:, j % 3], mx1[:, j % 3], -SM_SCALE, None, ALU.mult).then_inc(s["mla_max"], 1)

            def mla_norm(j):
                nk = TR * (j // NH + 1)
                dve.wait_ge(s["mla_exp"], j + 1)
                step(v.reciprocal(rrec[:, j % 3], rsum[:, j % 3]))
                v.tensor_scalar(sbuf_s[j % 3][:, 0:nk], sbuf_s[j % 3][:, 0:nk], rrec[:, j % 3], None, ALU.mult)\
                    .then_inc(s["mla_p"], 1)

            def mla_copy(j):
                dve.wait_ge(s["mla_o"], j + 1)
                v.tensor_copy(olT[:, j % NH, tile(j // NH)], ps[:, 6 + j % 2, 0:TR]).then_inc(s["mla_done"], 1)

            dve.wait_ge(s["dg_ps"], TI)
            dve.wait_ge(s["z_done"], 28)
            for j in range(NJ + 4):
                if j < NJ:
                    mla_max(j)
                if 1 <= j <= NJ:
                    mla_norm(j - 1)
                if j >= 4:
                    mla_copy(j - 4)
            dve.wait_ge(s["inter_ps"], 1)
            v.tensor_copy(numT, ps[:, 6, 0:128].rearrange("p (h t) -> p h t", h=MH)).then_inc(s["numt_done"], 1)
            step(v.tensor_tensor(nq, ps[0:NS, 6, 256:288].rearrange("p (h b) -> p h b", h=MH),
                                 bc(const("selb", rows=NS), 1, MH), ALU.mult))
            step(v.tensor_reduce(nqs, nq, AX, ALU.add))
            dve.wait_ge(s["numi_ps"], 1)
            v.tensor_copy(numi, ps[0:NS, 7, :].rearrange("p (h v) -> p h v", h=MH)).then_inc(s["inter_done"], 1)
            dve.wait_ge(s["csbc_done"], TI)
            m0 = const("m0", TI, MH, rows=TR)
            for i in range(TI):
                nk = TR * (i + 1)
                if i >= 1:
                    dve.wait_ge(s["ml_tps"], MH * i)
                for h in range(MH):
                    ins = v.tensor_tensor_reduce(wexp[:, h, 0:nk], cs_bc[0:TR, h, 0:nk], mask[:, i, 0:nk], 1.0, -3e38,
                                                 ALU.add, ALU.max, mx4[:, h:h + 1])
                step(ins)
                step(v.tensor_tensor(mm[:, i, :], mx4, m0[:, i, :], ALU.max))
                v.tensor_scalar(nm[:, i, :], mm[:, i, :], -1.0, None, ALU.mult)
                v.tensor_tensor(mabs[:, i, :], cum[:, i, :], mm[:, i, :], ALU.add)
                v.tensor_tensor(am[:, i, :], m0[:, i, :], mm[:, i, :], ALU.subtract).then_inc(s["ml_m"], 1)
                for h in range(MH):
                    n = i * MH + h
                    dve.wait_ge(s["ml_w"], (MH + 1) * i + h + 1)
                    dve.wait_ge(s["ml_qk"], n + 1)
                    src = ps[0:TR, 2 * (n % 2):2 * (n % 2) + 2, :].rearrange("p a b -> p (a b)")[:, 0:nk]
                    v.tensor_tensor_reduce(wexp[:, h, 0:nk], src, wexp[:, h, 0:nk], 1.0, 0.0, ALU.mult, ALU.add,
                                           den[:, h:h + 1]).then_inc(s["ml_p"], 1)
                dve.wait_ge(s["ml_p"], MH * (i + 1))
                dve.wait_ge(s["ml_w"], (MH + 1) * (i + 1))
                if i == 0:
                    step(v.tensor_tensor(nqs, nqs, am[0:NS, 0, :], ALU.mult))
                    v.tensor_tensor(numi, numi, bc(am[0:NS, 0, :], 2, DH), ALU.mult)
                    step(v.tensor_tensor(den[0:NS], den[0:NS], nqs, ALU.add))
                step(v.scalar_tensor_tensor(den, den, -1.0, den, ALU.mult, ALU.max))
                step(v.tensor_tensor(den, den, emm[:, i, :], ALU.max))
                step(v.reciprocal(rden, den))
                dve.wait_ge(s["ml_num"], MH * (i + 1))
                num = ps[0:TR, 6, :].rearrange("p (h v) -> p h v", h=MH)
                if i == 0:
                    step(v.tensor_copy(hbuf, num))
                    step(v.tensor_tensor(hbuf[0:NS], hbuf[0:NS], numi, ALU.add))
                    num = hbuf
                v.tensor_tensor(hbuf, num, bc(rden, 2, DH), ALU.mult).then_inc(s["ml_h"], 1)
                dve.wait_ge(s["ml_h"], i + 1)
                for h in range(MH):
                    ins = v.bn_stats(st6[:, h, :], hbuf[:, h, :])
                step(ins)
                for h in range(MH):
                    ins = v.bn_aggr(mvh[:, h, :], st6[:, h:h + 1, :])
                step(ins)
                v.tensor_scalar(rs4, mvh[:, :, 1], 1e-5, None, ALU.add).then_inc(s["hvar"], 1)
                dve.wait_ge(s["hstd"], i + 1)
                step(v.reciprocal(rs4, rs4))
                for h in range(MH):
                    ins = v.tensor_scalar(hbuf[:, h, :], hbuf[:, h, :], mvh[:, h, 0:1], rs4[:, h:h + 1],
                                          ALU.subtract, ALU.mult)
                step(ins)
                hf = hbuf.rearrange("p h v -> p (h v)")
                step(v.tensor_tensor(hf, hf, const("mhg", rows=TR), ALU.mult))
                v.tensor_tensor(zo[:, i, :], zo[:, i, :], hf, ALU.mult).then_inc(s["ml_gated"], 1)
            dve.wait_ge(s["mlast_ps"], 1)
            v.tensor_copy(mlast, ps[0:NS, 7, 8:8 + MH])
            step(v.tensor_copy(nml, ps[:, 7, 0:MH]))
            v.tensor_tensor(wsp, cs, bc(nml[0:TR, :], 1, TI), ALU.subtract).then_inc(s["ws_lin"], 1)
            v.tensor_tensor(wss, cs[0:NS, 0, :], mlast, ALU.subtract).then_inc(s["sws_lin"], 1)
            dve.wait_ge(s["ml_pt"], TI * MH)
            v.tensor_tensor(sR, bc(am[0:NS, 0, :], 2, SB), bc(const("lastb", rows=NS), 1, MH), ALU.mult).then_inc(s["sel_ready"], 1)
            dve.wait_ge(s["ws_exp"], 1)
            v.tensor_scalar(wsp[:, 0, :], wsp[:, 0, :], const("pmask", rows=TR), None, ALU.mult).then_inc(s["wsp_done"], 1)
            dve.wait_ge(s["wsp_done"], 1)
            for i in range(TI):
                if i >= 2:
                    dve.wait_ge(s["cst_ps"], i - 1)
                v.tensor_tensor(vw[:, i % 2].rearrange("p (h v) -> p h v", h=MH),
                                zv[:, i, :].rearrange("p (h v) -> p h v", h=MH), bc(wsp[:, i, :], 2, DH), ALU.mult)\
                    .then_inc(s["vw_ready"], 1)
            dve.wait_ge(s["cst_ps"], TI)
            dve.wait_ge(s["ml_num"], TI * MH)
            v.tensor_copy(cst[:, 0:512], ps[:, 0, :])
            v.tensor_copy(cst[:, 512:516], ps[:, 1, 0:MH]).then_inc(s["cst_done"], 1)
            dve.wait_ge(s["sws_exp"], 1)
            v.tensor_tensor(wsb, bc(wss, 2, SB), bc(const("selb", rows=NS), 1, MH), ALU.mult).then_inc(s["wsb_done"], 1)
            dve.wait_ge(s["wsb_done"], 1)
            dve.wait_ge(s["sel_ps"], 1)
            step(v.tensor_copy(aLb, ps[:, 7, 16:48]))
            nf = nst.rearrange("p h b -> p (h b)")
            dve.wait_ge(s["sst_ps"], 1)
            step(v.tensor_tensor(nf, nf, aLb, ALU.mult))
            v.tensor_tensor(nf, nf, ps[:, 6, 0:32], ALU.add).then_inc(s["sst_done"], 1)

            def state_values(b):
                if b >= 2:
                    dve.wait_ge(s["sst_ps"], b)
                v.tensor_tensor(vw[0:NS, b % 2].rearrange("p (h v) -> p h v", h=MH),
                                zv[0:NS, 0, :].rearrange("p (h v) -> p h v", h=MH), bc(wsb[:, :, b], 2, DH), ALU.mult)\
                    .then_inc(s["vwb_ready"], 1)

            state_values(0)
            for b in range(SB):
                if b + 1 < SB:
                    state_values(b + 1)
                dve.wait_ge(s["sst_ps"], b + 2)
                for h in range(MH):
                    c = h * SB + b
                    ins = v.scalar_tensor_tensor(ct[:, c, :], ct[:, c, :], aLb[:, c:c + 1],
                                                 ps[:, 2 + b % 2, h * 128:(h + 1) * 128], ALU.mult, ALU.add)
                ins.then_inc(s["sst_done"], 1)
            dve.wait_ge(s["ml_tps"], TI * MH)

            def sm_max(b):
                dve.wait_ge(s["sm_s"], b + 1)
                if b >= 1:
                    dve.wait_ge(s["sm_tps"], b)
                v.tensor_reduce(smx[:, 0:1], ps[0:NS, 0:4, :].rearrange("p a b -> p (a b)"), AX, ALU.max)
                step(v.tensor_tensor_reduce(s_p[:, 2048:2080], ps[0:NS, 4, 0:NS], smask[:, b, :], 1.0, -3e38,
                                            ALU.add, ALU.max, smx[:, 1:2]))
                step(v.tensor_tensor(smx[:, 2:3], smx[:, 0:1], smx[:, 1:2], ALU.max))
                v.tensor_scalar(smx[:, 2:3], smx[:, 2:3], -SM_SCALE, None, ALU.mult).then_inc(s["sm_max"], 1)

            sm_max(0)
            for b in range(SB):
                dve.wait_ge(s["sm_exp"], b + 1)
                step(v.tensor_tensor(smx[:, 0:1], smx[:, 0:1], smx[:, 1:2], ALU.add))
                step(v.reciprocal(smx[:, 1:2], smx[:, 0:1]))
                v.tensor_scalar(s_p, s_p, smx[:, 1:2], None, ALU.mult).then_inc(s["sm_p"], 1)
                dve.wait_ge(s["sm_p"], b + 1)
                if b + 1 < SB:
                    sm_max(b + 1)
                dve.wait_ge(s["sm_o"], b + 1)
                v.tensor_copy(olT[:, :, 4 * b:4 * b + 4], ps[:, 7, 0:NS].rearrange("p (h t) -> p h t", h=NH)).then_inc(s["sm_done"], 1)
            dve.wait_ge(s["ln1_in"], 16)
            for i in range(TI):
                for n in range(2):
                    dve.wait_ge(s["wo_ps"], 2 * i + n + 1)
                    seg = hid[:, i, n * 512:(n + 1) * 512]
                    v.scalar_tensor_tensor(seg, seg, ALPHA, ps[0:TR, (2 * i + n) % 4, :], ALU.mult, ALU.add)\
                        .then_inc(s["res_done"], 1)
                dve.wait_ge(s["res_done"], 2 * i + 2)
                layer_norm(hid[:, i, :], i, TI + i, lnv[:, 0, :], lnv[:, 1, :])
            dve.wait_ge(s["ht_ps"], 2 * TI)
            for hp in range(2 * PH):
                dve.wait_ge(s["sc_ps"], hp + 1)
                b = 4 + 2 * (hp % 2)
                v.tensor_copy(sc[:, 0:4, hp, :], ps[0:TR, b, :].rearrange("p (i k) -> p i k", i=4))
                v.tensor_copy(sc[:, 4, hp, :], ps[0:TR, b + 1, 0:128]).then_inc(s["sc_done"], 1)

            def top16(quads):
                for vals, idx, src, scratch in quads:
                    ins = v.max(vals[:, 0:8], src)
                step(ins)
                for vals, idx, src, scratch in quads:
                    v.max_index(idx[:, 0:8], vals[:, 0:8], src)
                for vals, idx, src, scratch in quads:
                    ins = v.match_replace(scratch, vals[:, 0:8], src, -BIG)
                step(ins)
                for vals, idx, src, scratch in quads:
                    ins = v.max(vals[:, 8:16], scratch)
                step(ins)
                for vals, idx, src, scratch in quads:
                    ins = v.max_index(idx[:, 8:16], vals[:, 8:16], scratch)
                step(ins)

            def take_sums(n):
                dve.wait_ge(s["y_ps"], NK * (n + 1))
                for d, t0, m, bank, col in PIECES[n]:
                    seg = hT[:, d, T0[n] + t0:T0[n] + t0 + m]
                    ins = v.scalar_tensor_tensor(seg, seg, ALPHA, ps[:, bank, col:col + m], ALU.mult, ALU.add)
                ins.then_inc(s["y_done"], 1)

            def low_part(dst, src, high, done_high, n):
                dve.wait_ge(done_high, n)
                return v.tensor_tensor(dst[:, :], src[:, :], as32(high[:, :]), ALU.subtract)

            def gate_rows(p, tok, r, n, n_free):
                m = GTS[r // ROUNDS][p]
                if n_free is not None:
                    dve.wait_ge(s["g_ps"], n_free)
                e0 = (r % ROUNDS) * EC
                v.tensor_tensor(oheq[:, p, 0:m], bc(pickT[:, 1, bass.ds(tok, m)], 2, EC), bc(iota[:, e0:e0 + EC], 1, m),
                                ALU.is_equal).then_inc(s["e2_equal"], 1)
                dve.wait_ge(s["e2_equal"], n)
                for part in range(2):
                    ins = v.tensor_tensor(oh2[p][:, 0:m, part], oheq[:, p, 0:m], bc(pickT[:, 2 + part, bass.ds(tok, m)], 2, EC),
                                          ALU.mult)
                ins.then_inc(s["oh2_ready"], 1)

            def gate_sum(p, tok, r, n):
                m = GTS[r // ROUNDS][p]
                dve.wait_ge(s["g_high"], n)
                g = ps[:, 6:8, :].rearrange("p b c -> p (b c)")[:, 0:m * 2 * EC].rearrange("p (t a e) -> p t a e", t=m, a=2)
                dst = gm[r % 2][:, bass.ds(tok, m), :]
                v.tensor_tensor(dst, dst, g[:, :, 1], ALU.add).then_inc(s["g_done"], 1)

            def first_gates(i, k):
                if not 0 <= i < len(FIRST):
                    return
                _, a, b = FIRST[i]
                if k == 0:
                    dve.wait_ge(s["pk_done"], i + 1)
                g = 2 * a + k
                if 2 * a < g <= 2 * b:
                    gate_sum((g - 1) % 2, (g - 1) * GTS[0][0], 0, g)
                if g < 2 * b:
                    gate_rows(g % 2, g * GTS[0][0], 0, g + 1, g - 1 if g >= 2 else None)

            dve.wait_ge(s["sc_done"], 16)
            dve.wait_ge(s["wo_ps"], 2 * TI)
            for i in range(TI):
                for q0 in range(0, 2 * PH, 4):
                    if q0:
                        for k in range(3):
                            first_gates(i - 1, q0 // 4 * 3 - 3 + k)
                    top16([(sv[:, q, :], siu[:, q, :], sc[:, i, q, :], tks[:, q - q0, 0:NK]) for q in range(q0, q0 + 4)])
                v.tensor_copy(sif, siu)
                for h0 in range(0, PH, 4):
                    for k in range(3):
                        first_gates(i - 1, 9 + h0 // 4 * 3 + k)
                    for h in range(h0, h0 + 4):
                        ins = v.tensor_tensor(cand[:, h - h0].rearrange("p (a b) -> p a b", a=TOPK), bc(sv[:, 2 * h, :], 2, TOPK),
                                              bc(sv[:, 2 * h + 1, :], 1, TOPK), ALU.add)
                    step(ins)
                    top16([(cv[:, h, :], ciu[:, h, :], cand[:, h - h0], tks[:, h - h0]) for h in range(h0, h0 + 4)])
                if i == 0:
                    for p in range(2):
                        low_part(ul[p], uraw[p], uh[p], s["uh_done"], p + 1).then_inc(s["ul_done"], 1)
                    dve.wait_ge(s["xh_done"], 1)
                    w = slice(0, PT[0])
                    v.tensor_tensor(xl[:, :, w], hT[:, :, passes(0)], as32(xh[:, :, w]), ALU.subtract).then_inc(s["xl_done"], 1)
                step(v.tensor_copy(tsum, cv[:, :, 0]))
                v.tensor_tensor(cv, cv, bc(tsum, 2, TOPK), ALU.subtract).then_inc(s["tk_lin"], 1)
                cf = ciu.rearrange("p h k -> p (h k)")
                v.tensor_scalar(cau[:, 0], cf, 4, None, ALU.logical_shift_right)
                step(v.tensor_scalar(cau[:, 1], cf, 15, None, ALU.bitwise_and))
                step(v.tensor_copy(ca, cau))
                if i >= 1:
                    dve.wait_ge(s["pk_ps"], i)
                for p in range(2):
                    keys = sif.rearrange("p (h t) j -> p h t j", t=2)[:, :, p, :]
                    step(v.tensor_tensor(eq, bc(ca[:, p].rearrange("p (h k) -> p h k", h=PH), 3, TOPK),
                                         bc(bc(iota[0:TR, 0:TOPK], 1, TOPK), 1, PH), ALU.is_equal))
                    step(v.tensor_tensor(eq, eq, bc(keys, 2, TOPK), ALU.mult))
                    step(v.tensor_reduce(pick[:, p].rearrange("p (h k) -> p h k", h=PH), eq, AX, ALU.add))
                dve.wait_ge(s["tk_exp"], i + 1)
                step(v.tensor_reduce(tsum, cv, AX, ALU.add))
                step(v.reciprocal(tsum, tsum))
                step(v.tensor_tensor(pick[:, 2].rearrange("p (h k) -> p h k", h=PH), cv, bc(tsum, 2, TOPK), ALU.mult))
                step(v.tensor_copy(ghr[:, :], pick[:, 2]))
                step(v.tensor_tensor(pick[:, 3], pick[:, 2], as32(ghr[:, :]), ALU.subtract))
                v.tensor_copy(pick[:, 2], as32(ghr[:, :])).then_inc(s["tk_pick"], 1)

            def gate(p, e, r, n_a, n_free):
                dve.wait_ge(s["a_done"], n_a)
                if n_free is not None:
                    dve.wait_ge(s["y_ps"], n_free)
                w = slice(0, PT[r // ROUNDS])
                g = gm[r % 2][:, w, bass.ds(e, 1)].rearrange("p t a -> p (t a)")
                v.tensor_tensor(hh[p][:, w], ab[:, p, w], g, ALU.mult)
                v.tensor_tensor(hraw[:, p, w], ab[:, p, w], g, ALU.mult).then_inc(s["h_raw"], 1)
                dve.wait_ge(s["h_raw"], n_a)
                v.tensor_tensor(hl[p][:, w], hraw[:, p, w], as32(hh[p][:, w]), ALU.subtract).then_inc(s["h_done"], 1)

            dve.wait_ge(s["pk_done"], TI)
            low_part(vl[0], vraw[0], vh[0], s["vh_done"], 1).then_inc(s["vl_done"], 1)
            for r in range(2 * ROUNDS):
                b0 = r * EC
                if r == ROUNDS:
                    dve.wait_ge(s["xh_done"], 2)
                    w = slice(0, PT[1])
                    v.tensor_tensor(xl[:, :, w], hT[:, :, passes(1)], as32(xh[:, :, w]), ALU.subtract).then_inc(s["xl_done"], 1)
                    take_sums(0)
                dve.wait_ge(s["g_done"], b0 + EC)

                def block(j, p, n_free, last):
                    m = min((r + 1) // ROUNDS, 1)
                    tok = j * PAIR[m] + p * GTS[m][0]
                    if r < 2 * ROUNDS - 1:
                        gate_rows(p, tok + T0[m], r + 1, j * 2 + (b0 + EC + p + 1), j * 2 + (b0 + EC + p - 1))
                    gate(p, j * 2 + p, r, j * 2 + (b0 + p + 1), n_free)
                    if last < 2:
                        low_part(ul[p], uraw[p], uh[p], s["uh_done"], j * 2 + (b0 + p + 3)).then_inc(s["ul_done"], 1)
                    if r < 2 * ROUNDS - 1:
                        gate_sum(p, tok, r + 1, j * 2 + (b0 + EC + p + 1))
                    if last < 3:
                        low_part(vl[1 - p], vraw[1 - p], vh[1 - p], s["vh_done"], j * 2 + (b0 + p + 2)).then_inc(s["vl_done"], 1)

                start, end = int(r == 0), EC // 2 - int(r == 2 * ROUNDS - 1)
                if start:
                    for p in range(2):
                        block(0, p, None, 0)
                with dve.Fori(start, end) as j:
                    for p in range(2):
                        block(j, p, j * 2 + (b0 + p - 1), 0)
                if end < EC // 2:
                    for p in range(2):
                        block(end, p, b0 + EC - 3 + p, 2 + p)
            take_sums(1)
            dve.wait_ge(s["ln2_in"], 16)
            for i in range(TI):
                dve.wait_ge(s["yt_done"], i + 1)
                layer_norm(yt[:, i, :], i, 2 * TI + i, lnv2[:, 0, :], lnv2[:, 1, :])


def shape_constants():
    import numpy as np

    c = {k: np.zeros((128, n), np.float32) for k, n in CONSTS.items()}
    c["ident"][:] = np.eye(128)
    c["iota"][:] = np.arange(128)
    c["ones"][:] = 1
    t = np.arange(NT)
    seq = np.where(t < NS, t // SS, -1)
    may = (seq[:, None] == seq[None, :]) & (t[None, :] <= t[:, None])
    m = np.where(may, 0, -BIG).astype(np.float32).reshape(TI, TR, NT).transpose(1, 0, 2)
    c["mask"][:TR] = m.reshape(TR, -1)
    c["ltd0"][:TR] = may[:TR, :TR].T
    c["ltdc"][:TR] = np.triu(np.ones((TR, TR)))
    c["lt01"][NS:TR] = 1
    r = np.arange(NH * SS) % SS
    k = np.arange(NS)
    c["smask"][:NS] = np.stack([np.where((k[None] // SS == b) & (k[None] % SS <= r[:, None]), 0, -BIG)
                                for b in range(SB)], 1).reshape(NS, -1)
    c["sellast"][TR - 1] = 1
    c["lsel"][:NS] = (k[:, None] == (k[None] // SS) * SS + SS - 1)
    c["selb"][:NS] = k[:, None] // SS == np.arange(SB)[None]
    c["lastb"][:NS] = k[:, None] == np.arange(SB)[None] * SS + SS - 1
    c["pmask"][NS:] = 1
    past = PAGES * PAGE
    pos = np.concatenate([past + k % SS, np.arange(NPR)]).astype(np.float32)
    inv = np.float32(10000.0) ** (-np.arange(16, dtype=np.float32) / np.float32(16))
    ang = (pos[:, None] * inv.astype(np.float32)).astype(np.float32)
    for name, f in (("cos", np.cos), ("sin", np.sin)):
        c[name][:TR] = f(ang).astype(np.float32).reshape(TI, TR, 16).transpose(1, 0, 2).reshape(TR, -1)
    return np.concatenate([c[k] for k in CONSTS], axis=1)


def kernel(**inputs):
    import concourse.bacc as bacc
    import numpy as np
    from concourse.bass_utils import run_bass_kernel_spmd

    a = {k: np.asarray(v) for k, v in inputs.items()}

    def rows(*vs):
        return np.ascontiguousarray(np.stack([np.broadcast_to(v.reshape(-1), (128, v.size)) for v in vs], 1))

    def tiles(w):
        return w.reshape(-1, 128, w.shape[1]).transpose(1, 0, 2)

    x = np.concatenate([a["x_sample"].reshape(NS, D), a["meta_tokens"], a["x_prompt"].reshape(-1, D)])
    m0 = np.zeros((NT, MH), np.float32)
    m0[:NS] = np.repeat(a["state_m"][0], SS, axis=0)
    m0 = m0.reshape(TI, TR, MH).transpose(1, 0, 2).reshape(TR, -1)
    m0 = np.concatenate([m0, np.zeros((128 - TR, m0.shape[1]), np.float32)])
    vecs = np.concatenate([rows(a[n])[:, 0] for n in ("q_norm_g", "kv_norm_g", "mh_norm_g", "b_gates")] + [m0], axis=1)
    w = a["w_in"][0]
    o_kr, o_mq = QR + KVR, QR + KVR + ROPE
    mw = MH * DH
    z0w = np.concatenate([w[:, :o_mq], w[:, o_mq + 4 * mw:], np.zeros((D, 512 - Z0W), np.float32)], axis=1)
    order = [z0w] + [w[:, o_mq + n * mw:o_mq + (n + 1) * mw] for n in (1, 2, 3, 0)]
    w_in = np.stack([tiles(c) for c in order])
    qb = a["w_qb"][0].reshape(QR, NH, NOPE + ROPE)
    w_qb = tiles(np.concatenate([qb[:, :, :NOPE].reshape(QR, -1), qb[:, :, NOPE:].reshape(QR, -1)], axis=1))
    kvb = a["w_kvb"][0].reshape(KVR, NH, NOPE + VD)
    w_uk = kvb[:, :, :NOPE].transpose(1, 2, 0).reshape(4, 128, KVR).transpose(1, 0, 2)
    w_uv = kvb[:, :, NOPE:].reshape(KVR, -1)
    w_pq = a["w_pq"][0].reshape(KD, 128, 4, 512).transpose(2, 1, 0, 3)
    sub_keys = a["sub_keys"][0].reshape(16, NK, 128).transpose(2, 0, 1)
    eu = a["expert_u"][0].reshape(NK, NK, KD, 128).transpose(1, 3, 2, 0)
    ev = a["expert_v"][0].reshape(NK, NK, D).transpose(1, 0, 2)
    ckv_c = a["cache_ckv"][0]
    kpe_c = a["cache_kpe"][0].reshape(-1, 4, PAGE // 4, ROPE).transpose(0, 1, 3, 2).reshape(-1, 128, PAGE // 4)
    ins = dict(
        x=x, consts=shape_constants(), vecs=vecs, lnin=rows(a["ln_in_g"], a["ln_in_b"]),
        ln1=rows(a["ln1_g"], a["ln1_b"]), ln2=rows(a["ln2_g"], a["ln2_b"]), w_in=w_in, w_qb=w_qb, w_uk=w_uk, w_uv=w_uv,
        w_o=tiles(a["w_o"][0]), w_pq=w_pq, sub_keys=sub_keys, eu=eu, ev=ev,
        cache=np.concatenate([ckv_c, ckv_c.transpose(0, 2, 1), kpe_c], axis=2),
        pages=a["page_table"].reshape(1, -1).astype(np.int32),
        ct0=a["state_C"][0].transpose(3, 1, 0, 2).reshape(DH, MH * SB, DH), nt0=a["state_n"][0].transpose(2, 1, 0))
    outs = dict(o_y=(NT, D), o_ckv=(NT, KVR), o_kpe=(NT, ROPE), o_c=(DH, MH * DH), o_n=(DH, MH), o_m=(NT, MH),
                o_cs=(DH, MH * SB, DH), o_ns=(DH, MH, SB))
    nc = bacc.Bacc("TRN2", target_bir_lowering=False, num_devices=1)
    arrays, args = {}, []
    for name, v in ins.items():
        v = np.ascontiguousarray(v)
        arrays[name] = v
        args.append(nc.dram_tensor(name, v.shape, mybir.dt.from_np(v.dtype), kind="ExternalInput").ap())
    for name, shape in outs.items():
        args.append(nc.dram_tensor(name, shape, F32, kind="ExternalOutput").ap())
    build(nc, *args)
    r = run_bass_kernel_spmd(nc, [arrays], core_ids=[0]).results[0]
    y, ckv, kpe, m = r["o_y"], r["o_ckv"], r["o_kpe"], r["o_m"]
    c_p = r["o_c"].reshape(DH, MH, DH).transpose(1, 2, 0)
    c_s = r["o_cs"].reshape(DH, MH, SB, DH).transpose(2, 1, 3, 0)
    return (y[NS + 16:][None], y[:NS].reshape(SB, SS, D),
            ckv[NS:][None, None], kpe[NS:][None, None], np.ascontiguousarray(c_p)[None, None],
            np.ascontiguousarray(r["o_n"].T)[None, None], m[-1][None, None],
            ckv[:NS].reshape(1, SB, SS, KVR), kpe[:NS].reshape(1, SB, SS, ROPE), np.ascontiguousarray(c_s)[None],
            np.ascontiguousarray(r["o_ns"].transpose(2, 1, 0))[None], m[SS - 1:NS:SS][None])
```
